# Optimizing a Trainium2 kernel written in Bass

```python
import math
import jax, jax.numpy as jnp
from jax import lax
import numpy as np

D_MODEL = 1024
BATCH = 1
SEQ = 256
DEPTH = 2

MIX_WIDTH = D_MODEL
GROUP_WIDTH = MIX_WIDTH // 4
HEAD_DIM = 64
H_A = GROUP_WIDTH // HEAD_DIM
H_IDX = 4
D_IDX = 64
TOPK_MAX = 256
H_B = GROUP_WIDTH // HEAD_DIM
MLA_Q_RANK = 256
MLA_KV_RANK = 128
MLA_NOPE = 64
MLA_ROPE = 32
MLA_V = 64
ROPE_THETA = 10000.0
H_C = GROUP_WIDTH // HEAD_DIM
S5_GROUP_CH = 16
S5_GROUPS = GROUP_WIDTH // S5_GROUP_CH
S5_STATE = 64
REL_BUCKETS = 32
REL_MAX_DIST = 128
PEER_HEADS = 8
PEER_KEYS = 128
PEER_N = PEER_KEYS * PEER_KEYS
PEER_DKEY = 256
PEER_TOPK = 16
PEER_CHUNK = 128
Q_BLOCK = 128
EPS = 1e-6
IN_SIZES = (H_A * HEAD_DIM, H_A * HEAD_DIM, H_A * HEAD_DIM,
            H_IDX * D_IDX, D_IDX, H_IDX,
            MLA_Q_RANK, MLA_KV_RANK, MLA_ROPE,
            H_C * HEAD_DIM, H_C * HEAD_DIM, H_C * HEAD_DIM, H_C,
            GROUP_WIDTH)
IN_WIDTH = sum(IN_SIZES)

kernel_name = "hybrid_dsa_mla_fox_s5_peer_block"

def rmsnorm(x, g):
    xf = x.astype(jnp.float32)
    y = xf * lax.rsqrt(jnp.mean(xf * xf, axis=-1, keepdims=True) + EPS)
    return (y * g.astype(jnp.float32)).astype(x.dtype)

def rel_bucket(n):
    max_exact = REL_BUCKETS // 2
    n = jnp.maximum(n, 0)
    nf = jnp.maximum(n, 1).astype(jnp.float32)
    log_ratio = jnp.log(nf / max_exact) / math.log(REL_MAX_DIST / max_exact)
    large = max_exact + (log_ratio * (REL_BUCKETS - max_exact)).astype(jnp.int32)
    return jnp.where(n < max_exact, n, jnp.minimum(large, REL_BUCKETS - 1))

def rope(x, pos):
    half = x.shape[-1] // 2
    freqs = ROPE_THETA ** (-jnp.arange(half, dtype=jnp.float32) / half)
    ang = pos.astype(jnp.float32)[..., None] * freqs
    cos, sin = jnp.cos(ang)[:, :, None, :], jnp.sin(ang)[:, :, None, :]
    x1, x2 = x[..., :half], x[..., half:]
    return jnp.concatenate([x1 * cos - x2 * sin, x1 * sin + x2 * cos], axis=-1).astype(x.dtype)

def blocked_causal_attention(q, k, v, scale, bias_fn=None):
    S = q.shape[1]
    outs = []
    for i in range(S // Q_BLOCK):
        q0, q1 = i * Q_BLOCK, (i + 1) * Q_BLOCK
        logits = jnp.einsum('bqhd,bkhd->bhqk', q[:, q0:q1], k[:, :q1]).astype(jnp.float32) * scale
        if bias_fn is not None:
            logits = logits + bias_fn(q0, q1)
        causal = (q0 + jnp.arange(Q_BLOCK))[:, None] >= jnp.arange(q1)[None, :]
        logits = jnp.where(causal, logits, -jnp.inf)
        p = jax.nn.softmax(logits, axis=-1).astype(v.dtype)
        outs.append(jnp.einsum('bhqk,bkhd->bqhd', p, v[:, :q1]))
    return jnp.concatenate(outs, axis=1)

def dsa_attention(q, k, v, q_idx, k_idx, w_idx, positions, rel_bias):
    S = q.shape[1]
    topk = min(TOPK_MAX, S // 4)
    scale = HEAD_DIM ** -0.5
    gather = jax.vmap(lambda table, idx: table[idx])
    outs = []
    for i in range(S // Q_BLOCK):
        q0, q1 = i * Q_BLOCK, (i + 1) * Q_BLOCK
        kk = min(topk, q1)
        tq = q0 + jnp.arange(Q_BLOCK)
        causal = tq[:, None] >= jnp.arange(q1)[None, :]
        dots = jnp.einsum('bqhd,bkd->bqhk', q_idx[:, q0:q1], k_idx[:, :q1])
        score = jnp.einsum('bqh,bqhk->bqk', w_idx[:, q0:q1], jax.nn.relu(dots)).astype(jnp.float32)
        score = jnp.where(causal, score, -jnp.inf)
        _, sel = lax.top_k(score, kk)
        valid = sel <= tq[None, :, None]
        k_sel = gather(k, sel)
        v_sel = gather(v, sel)
        dist = positions[:, q0:q1, None] - gather(positions, sel)
        bias = jnp.swapaxes(rel_bias[rel_bucket(dist)], -1, -2)
        logits = (jnp.einsum('bqhd,bqkhd->bqhk', q[:, q0:q1], k_sel).astype(jnp.float32) * scale
                  + bias.astype(jnp.float32))
        logits = jnp.where(valid[:, :, None, :], logits, -jnp.inf)
        p = jax.nn.softmax(logits, axis=-1).astype(v.dtype)
        outs.append(jnp.einsum('bqhk,bqkhd->bqhd', p, v_sel))
    return jnp.concatenate(outs, axis=1)

def mla_attention(cq, ckv, kr, q_norm_g, kv_norm_g, w_uq, w_ukv, positions):
    B, S, _ = cq.shape
    q = (rmsnorm(cq, q_norm_g) @ w_uq).reshape(B, S, H_B, MLA_NOPE + MLA_ROPE)
    kv = (rmsnorm(ckv, kv_norm_g) @ w_ukv).reshape(B, S, H_B, MLA_NOPE + MLA_V)
    q = jnp.concatenate([q[..., :MLA_NOPE], rope(q[..., MLA_NOPE:], positions)], axis=-1)
    k_rope = jnp.broadcast_to(rope(kr[:, :, None, :], positions), (B, S, H_B, MLA_ROPE))
    k = jnp.concatenate([kv[..., :MLA_NOPE], k_rope], axis=-1)
    v = kv[..., MLA_NOPE:]
    return blocked_causal_attention(q, k, v, (MLA_NOPE + MLA_ROPE) ** -0.5)

def forgetting_attention(q, k, v, f_logit, b_f):
    log_f = jax.nn.log_sigmoid(f_logit.astype(jnp.float32) + b_f.astype(jnp.float32))
    cum = jnp.swapaxes(jnp.cumsum(log_f, axis=1), 1, 2)

    def bias_fn(q0, q1):
        return cum[:, :, q0:q1, None] - cum[:, :, None, :q1]

    return blocked_causal_attention(q, k, v, HEAD_DIM ** -0.5, bias_fn)

def _complex_scan_combine(e1, e2):
    a1r, a1i, b1r, b1i = e1
    a2r, a2i, b2r, b2i = e2
    return (a2r * a1r - a2i * a1i,
            a2r * a1i + a2i * a1r,
            a2r * b1r - a2i * b1i + b2r,
            a2r * b1i + a2i * b1r + b2i)

def s5_layer(u, A_re, A_im, log_dt, B_re, B_im, C_re, C_im, D, w_glu, b_glu):
    Bsz, S, _ = u.shape
    f32 = jnp.float32
    u32 = u.astype(f32)
    ug = u32.reshape(Bsz, S, S5_GROUPS, S5_GROUP_CH)
    lam_re, lam_im = A_re.astype(f32), A_im.astype(f32)
    dt = jnp.exp(log_dt.astype(f32))[:, None]
    mag = jnp.exp(lam_re * dt)
    a_re, a_im = mag * jnp.cos(lam_im * dt), mag * jnp.sin(lam_im * dt)
    den = lam_re * lam_re + lam_im * lam_im
    coef_re = ((a_re - 1.0) * lam_re + a_im * lam_im) / den
    coef_im = (a_im * lam_re - (a_re - 1.0) * lam_im) / den
    Br, Bi = B_re.astype(f32), B_im.astype(f32)
    bb_re = coef_re[..., None] * Br - coef_im[..., None] * Bi
    bb_im = coef_re[..., None] * Bi + coef_im[..., None] * Br
    bu_re = jnp.einsum('bsgh,gph->bsgp', ug, bb_re)
    bu_im = jnp.einsum('bsgh,gph->bsgp', ug, bb_im)
    elems = (jnp.broadcast_to(a_re, bu_re.shape), jnp.broadcast_to(a_im, bu_im.shape), bu_re, bu_im)
    _, _, x_re, x_im = lax.associative_scan(_complex_scan_combine, elems, axis=1)
    y = (jnp.einsum('bsgp,ghp->bsgh', x_re, C_re.astype(f32))
         - jnp.einsum('bsgp,ghp->bsgh', x_im, C_im.astype(f32)))
    y = y.reshape(Bsz, S, GROUP_WIDTH) + D.astype(f32) * u32
    g = jax.nn.gelu(y)
    out = g * jax.nn.sigmoid(g @ w_glu.astype(f32) + b_glu.astype(f32))
    return out.astype(u.dtype)

def hybrid_mixer(h, positions, rel_bias, w_in, mla_q_norm_g, mla_kv_norm_g, mla_w_uq, mla_w_ukv,
                 fox_b_f, s5_A_re, s5_A_im, s5_log_dt, s5_B_re, s5_B_im, s5_C_re, s5_C_im, s5_D,
                 s5_w_glu, s5_b_glu, group_norm_g, w_out):
    B, S, _ = h.shape
    proj = h @ w_in
    cuts = [int(v) for v in np.cumsum(IN_SIZES)[:-1]]
    (a_q, a_k, a_v, i_q, i_k, i_w, b_cq, b_ckv, b_kr,
     c_q, c_k, c_v, c_f, d_u) = jnp.split(proj, cuts, axis=-1)

    def heads(t, n):
        return t.reshape(B, S, n, -1)

    y_a = dsa_attention(heads(a_q, H_A), heads(a_k, H_A), heads(a_v, H_A),
                        heads(i_q, H_IDX), i_k, i_w, positions, rel_bias)
    y_b = mla_attention(b_cq, b_ckv, b_kr, mla_q_norm_g, mla_kv_norm_g, mla_w_uq, mla_w_ukv, positions)
    y_c = forgetting_attention(heads(c_q, H_C), heads(c_k, H_C), heads(c_v, H_C), c_f, fox_b_f)
    y_d = s5_layer(d_u, s5_A_re, s5_A_im, s5_log_dt, s5_B_re, s5_B_im, s5_C_re, s5_C_im, s5_D,
                   s5_w_glu, s5_b_glu)
    groups = jnp.stack([y_a.reshape(B, S, GROUP_WIDTH), y_b.reshape(B, S, GROUP_WIDTH),
                        y_c.reshape(B, S, GROUP_WIDTH), y_d], axis=2)
    groups = rmsnorm(groups, group_norm_g.reshape(4, GROUP_WIDTH))
    return groups.reshape(B, S, MIX_WIDTH) @ w_out

def peer_ffn(h, w_q, sk1, sk2, u_tab, v_tab):
    B, S, Dm = h.shape
    t = h.reshape(-1, Dm)
    T = t.shape[0]
    q = (t @ w_q).reshape(T, PEER_HEADS, 2, PEER_DKEY // 2)
    s1 = jnp.einsum('thd,kd->thk', q[:, :, 0], sk1).astype(jnp.float32)
    s2 = jnp.einsum('thd,kd->thk', q[:, :, 1], sk2).astype(jnp.float32)
    v1, i1 = lax.top_k(s1, PEER_TOPK)
    v2, i2 = lax.top_k(s2, PEER_TOPK)
    cand = (v1[..., :, None] + v2[..., None, :]).reshape(T, PEER_HEADS, PEER_TOPK * PEER_TOPK)
    vc, ic = lax.top_k(cand, PEER_TOPK)
    expert = (jnp.take_along_axis(i1, ic // PEER_TOPK, axis=-1) * PEER_KEYS
              + jnp.take_along_axis(i2, ic % PEER_TOPK, axis=-1))
    gate = jax.nn.softmax(vc, axis=-1)

    def chunk(args):
        tc, ec, gc = args
        a = jnp.einsum('td,thkd->thk', tc, u_tab[ec]).astype(jnp.float32)
        w = (gc * jax.nn.gelu(a)).astype(tc.dtype)
        return jnp.einsum('thk,thkd->td', w, v_tab[ec])

    n_chunks = T // PEER_CHUNK
    y = lax.map(chunk, (t.reshape(n_chunks, PEER_CHUNK, Dm),
                        expert.reshape(n_chunks, PEER_CHUNK, PEER_HEADS, PEER_TOPK),
                        gate.reshape(n_chunks, PEER_CHUNK, PEER_HEADS, PEER_TOPK)))
    return y.reshape(B, S, Dm)

def setup_inputs(seed: int = 0) -> dict:
    key = jax.random.key(seed)
    keys = jax.random.split(key, 40)
    counter = [0]
    f32 = jnp.float32

    def nk():
        k = keys[counter[0]]
        counter[0] += 1
        return k

    def nrm(shape, scale):
        return jax.random.normal(nk(), shape, f32) * scale

    def gain(shape):
        return 1.0 + nrm(shape, 0.05)

    L = DEPTH
    x = nrm((BATCH, SEQ, D_MODEL), 1.0)
    c = nrm((BATCH, D_MODEL), 1.0)
    offs = jax.random.randint(nk(), (BATCH, 1), 0, 1024, dtype=jnp.int32)
    positions = offs + jnp.arange(SEQ, dtype=jnp.int32)[None, :]
    rel_bias = nrm((REL_BUCKETS, H_A), 0.5)
    ada_w = nrm((L, D_MODEL, 6 * D_MODEL), 0.5 * D_MODEL ** -0.5)
    ada_b = nrm((L, 6 * D_MODEL), 0.01)
    norm1_g = gain((L, D_MODEL))
    w_in = nrm((L, D_MODEL, IN_WIDTH), D_MODEL ** -0.5)
    mla_q_norm_g = gain((L, MLA_Q_RANK))
    mla_kv_norm_g = gain((L, MLA_KV_RANK))
    mla_w_uq = nrm((L, MLA_Q_RANK, H_B * (MLA_NOPE + MLA_ROPE)), MLA_Q_RANK ** -0.5)
    mla_w_ukv = nrm((L, MLA_KV_RANK, H_B * (MLA_NOPE + MLA_V)), MLA_KV_RANK ** -0.5)
    fox_b_f = jax.random.uniform(nk(), (L, H_C), f32, 1.0, 4.0)
    s5_A_re = -0.5 + nrm((L, S5_GROUPS, S5_STATE), 0.01)
    s5_A_im = jnp.pi * jnp.arange(S5_STATE, dtype=f32) + nrm((L, S5_GROUPS, S5_STATE), 0.01)
    s5_log_dt = jax.random.uniform(nk(), (L, S5_GROUPS), f32, math.log(1e-3), math.log(1e-1))
    s5_B_re = nrm((L, S5_GROUPS, S5_STATE, S5_GROUP_CH), S5_GROUP_CH ** -0.5)
    s5_B_im = nrm((L, S5_GROUPS, S5_STATE, S5_GROUP_CH), S5_GROUP_CH ** -0.5)
    s5_C_re = nrm((L, S5_GROUPS, S5_GROUP_CH, S5_STATE), S5_STATE ** -0.5)
    s5_C_im = nrm((L, S5_GROUPS, S5_GROUP_CH, S5_STATE), S5_STATE ** -0.5)
    s5_D = nrm((L, GROUP_WIDTH), 1.0)
    s5_w_glu = nrm((L, GROUP_WIDTH, GROUP_WIDTH), GROUP_WIDTH ** -0.5)
    s5_b_glu = nrm((L, GROUP_WIDTH), 0.01)
    group_norm_g = gain((L, MIX_WIDTH))
    w_out = nrm((L, MIX_WIDTH, D_MODEL), MIX_WIDTH ** -0.5)
    norm2_g = gain((L, D_MODEL))
    peer_w_q = nrm((L, D_MODEL, PEER_HEADS * PEER_DKEY), D_MODEL ** -0.5)
    peer_subkeys1 = nrm((L, PEER_KEYS, PEER_DKEY // 2), (PEER_DKEY // 2) ** -0.5)
    peer_subkeys2 = nrm((L, PEER_KEYS, PEER_DKEY // 2), (PEER_DKEY // 2) ** -0.5)
    peer_u = nrm((L, PEER_N, D_MODEL), D_MODEL ** -0.5)
    peer_v = nrm((L, PEER_N, D_MODEL), 1.0)
    final_g = gain((D_MODEL,))
    return {"x": x, "c": c, "positions": positions, "rel_bias": rel_bias,
            "ada_w": ada_w, "ada_b": ada_b, "norm1_g": norm1_g, "w_in": w_in,
            "mla_q_norm_g": mla_q_norm_g, "mla_kv_norm_g": mla_kv_norm_g,
            "mla_w_uq": mla_w_uq, "mla_w_ukv": mla_w_ukv, "fox_b_f": fox_b_f,
            "s5_A_re": s5_A_re, "s5_A_im": s5_A_im, "s5_log_dt": s5_log_dt,
            "s5_B_re": s5_B_re, "s5_B_im": s5_B_im, "s5_C_re": s5_C_re, "s5_C_im": s5_C_im,
            "s5_D": s5_D, "s5_w_glu": s5_w_glu, "s5_b_glu": s5_b_glu,
            "group_norm_g": group_norm_g, "w_out": w_out, "norm2_g": norm2_g,
            "peer_w_q": peer_w_q, "peer_subkeys1": peer_subkeys1, "peer_subkeys2": peer_subkeys2,
            "peer_u": peer_u, "peer_v": peer_v, "final_g": final_g}

def reference(x, c, positions, rel_bias, ada_w, ada_b, norm1_g, w_in, mla_q_norm_g, mla_kv_norm_g,
              mla_w_uq, mla_w_ukv, fox_b_f, s5_A_re, s5_A_im, s5_log_dt, s5_B_re, s5_B_im,
              s5_C_re, s5_C_im, s5_D, s5_w_glu, s5_b_glu, group_norm_g, w_out, norm2_g,
              peer_w_q, peer_subkeys1, peer_subkeys2, peer_u, peer_v, final_g):
    for l in range(DEPTH):
        mod = jax.nn.silu(c) @ ada_w[l] + ada_b[l]
        sh1, sc1, g1, sh2, sc2, g2 = jnp.split(mod[:, None, :], 6, axis=-1)
        h = rmsnorm(x, norm1_g[l]) * (1.0 + sc1) + sh1
        x = x + g1 * hybrid_mixer(h, positions, rel_bias, w_in[l], mla_q_norm_g[l], mla_kv_norm_g[l],
                                  mla_w_uq[l], mla_w_ukv[l], fox_b_f[l], s5_A_re[l], s5_A_im[l],
                                  s5_log_dt[l], s5_B_re[l], s5_B_im[l], s5_C_re[l], s5_C_im[l],
                                  s5_D[l], s5_w_glu[l], s5_b_glu[l], group_norm_g[l], w_out[l])
        h = rmsnorm(x, norm2_g[l]) * (1.0 + sc2) + sh2
        x = x + g2 * peer_ffn(h, peer_w_q[l], peer_subkeys1[l], peer_subkeys2[l], peer_u[l], peer_v[l])
    return rmsnorm(x, final_g)


_drawn_inputs = setup_inputs


def setup_inputs(seed=0):
    import zlib

    import numpy as np

    out = dict(_drawn_inputs(seed))
    spreads = {}
    factors = {'mla_q_norm_g': 2.748, 's5_A_re': 8.0, 's5_b_glu': 5.42}
    for name, (base, spread) in spreads.items():
        noise = np.random.default_rng([zlib.crc32(name.encode()), seed]).standard_normal(out[name].shape)
        drawn = base * np.exp(spread * noise) if base else spread * noise
        out[name] = __import__('jax').numpy.asarray(drawn.astype(out[name].dtype))
    for name, factor in factors.items():
        out[name] = (out[name] * factor).astype(out[name].dtype)
    return out
```

```python
from contextlib import ExitStack

import numpy as np

import concourse.bass as bass
from concourse import mybir

F32 = mybir.dt.float32
I32 = mybir.dt.int32
U32 = mybir.dt.uint32
ALU = mybir.AluOpType
ACT = mybir.ActivationFunctionType
AX_X = mybir.AxisListType.X

P = 128
DEPTH = 2
D = 1024
KT = D // P
T = 256
TT = T // P
GW = 256
HEADS = 4
HD = 64
KV_RANK = 128
NOPE = 64
ROPE = 32
EPS = 1e-6
TOPK = 64
BUCKETS = 32
MAX_DIST = 128
NS5 = 8
C5 = 32
PH = 8
PK = 16
KEYS = 128
BIG = 1.0e30
TAKEN = -3.0e38
BLOCK = KT * P
RING = 8

IN_NAMES = ["a_q", "a_k", "a_v", "i_q", "i_k", "i_w", "b_cq", "b_ckv", "b_kr", "c_q", "c_k", "c_v", "c_f", "d_u"]
IN_SIZES = [GW, GW, GW, HEADS * HD, HD, HEADS, GW, KV_RANK, ROPE, GW, GW, GW, HEADS, GW]
IN_AT = dict(zip(IN_NAMES, [(int(e - s), int(e)) for e, s in zip(np.cumsum(IN_SIZES), IN_SIZES)]))

PERM = [0, 2, 1, 3]

MIX_BLOCKS = ["du0", "du1", "iq0", "iq1", "ik", "B0", "aq0", "aq1", "ak0", "ak1", "B1", "av0", "av1",
              "cq0", "cq1", "ckv", "kr", "fq0", "fq1", "fk0", "fk1", "fv0", "fv1", "UQ", "UKV"]
ADA = 6 * KT
PQ = 2 * PH
LAYER_BLOCKS = ADA + len(MIX_BLOCKS) + KT + PQ + 2 * KEYS
N_BLOCKS = DEPTH * LAYER_BLOCKS

REGIONS = [("ss1", "act")]
REGIONS += [(n, "act") for n in ["du0", "du1", "iq0", "iq1", "ik", "aq0", "aq1", "ak0", "ak1", "av0", "av1", "iwcf",
                                 "cq0", "cq1", "ckv", "krA", "krB", "fq0", "fq1", "fk0", "fk1", "fv0", "fv1",
                                 "ssq", "sskv", "fcum"]]
REGIONS += [(f"qB{h}", "dve") for h in range(HEADS)] + [(f"kB{h}", "act") for h in range(HEADS)]
REGIONS += [("vB0", "act"), ("vB1", "act")]
REGIONS += [("y5_0", "dve"), ("y5_1", "dve"), ("glu0", "act"), ("glu1", "act"), ("ss5", "act")]
REGIONS += [(f"yt{n}", "act") for n in range(6)]
REGIONS += [(f"out{m}", "dve") for m in range(KT)] + [("ss2", "act")]
for _h in range(PH):
    REGIONS += [(f"pq{_h}_0", "act"), (f"pq{_h}_1", "act"), (f"sc{_h}_0", "act"), (f"sc{_h}_1", "act")]
REGIONS += [(f"tr{i}", "act") for i in range(3 * TT)]
N_REG = len(REGIONS)
REG_POS = {n: i for i, (n, _) in enumerate(REGIONS)}
PER_TAKER = {w: sum(t == w for _, t in REGIONS) for w in ("act", "dve")}


def taken_count(layer, name):
    i = REG_POS[name]
    w = REGIONS[i][1]
    return w, layer * PER_TAKER[w] + sum(t == w for _, t in REGIONS[:i + 1])


def columns(sizes):
    at, out = 0, {}
    for name, n in sizes:
        out[name] = (at, at + n)
        at += n
    return out, at


CONST_AT, N_CONST = columns([("ident", P), ("ones", P), ("utri", TT * T), ("causal", P + T), ("iota", P), ("time", T),
                             ("freq", 3), ("phase", 3), ("mul", 3), ("thr", BUCKETS - 1), ("neghalf", TT)])
SMALL_AT, N_SMALL = columns([("n1g", KT), ("n2g", KT), ("adab", ADA), ("qg", 2), ("kvg", 1), ("gng", KT), ("lre", NS5),
                             ("lim", NS5), ("ldt", NS5), ("D", 2), ("bglu", 2), ("iwcf", KT * 8), ("bf", HEADS),
                             ("sk1", P), ("sk2", P)])
VEC_AT, N_VEC = columns([("c", KT), ("fg", KT), ("rel", BUCKETS * HEADS)])

INV2PI = float(np.float32(1 / (2 * np.pi)))
TWOPI = 6.283185
PI = 3.1415925
MAGIC = 12582912.0
C1 = 6.28125
C2 = float(np.float32(np.round((2 * np.pi - C1) * 2 ** 20) / 2 ** 20))
C3 = float(np.float32(2 * np.pi - C1 - C2))


def constants():
    k = np.zeros((P, N_CONST), np.float32)

    def put(name, v):
        k[:, CONST_AT[name][0]:CONST_AT[name][1]] = v
    p = np.arange(P)
    t = np.arange(T)
    put("ident", np.eye(P))
    put("ones", 1.0)
    put("utri", np.concatenate([(p[:, None] + P * j <= t[None, :]) for j in range(TT)], axis=1))
    put("causal", np.concatenate([np.where(p[:, None] >= p[None, :], 0.0, -BIG),
                                  np.where(P + p[:, None] >= t[None, :], 0.0, -BIG)], axis=1))
    put("iota", p[None, :])
    put("time", t[None, :])
    half = ROPE // 2
    f = (np.float32(10000.0) ** (-(np.arange(half, dtype=np.float32)) / np.float32(half))).astype(np.float32)
    rows = f[p % half]
    scale = (NOPE + ROPE) ** -0.5
    sign = np.where(p % ROPE < half, -1.0, 1.0)
    put("freq", np.stack([np.where(p < NOPE, 0.0, rows), rows, rows], axis=1))
    put("phase", np.stack([np.where(p < NOPE + ROPE, np.pi / 2, 0.0), np.full(P, np.pi / 2), np.zeros(P)], axis=1))
    put("mul", np.stack([np.where(p < NOPE + ROPE, scale, scale * sign), np.ones(P), sign], axis=1))
    exact = BUCKETS // 2
    thr = [b if b < exact else int(np.ceil(exact * (MAX_DIST / exact) ** ((b - exact) / (BUCKETS - exact)) - 1e-9))
           for b in range(1, BUCKETS)]
    put("thr", np.array(thr)[None, :])
    put("neghalf", -0.5)
    return k


def build(nc, stream, s5w, consts, small, vec, pos, x_in, out):
    with ExitStack() as ctx:
        def sb(name, shape, dt=F32):
            return ctx.enter_context(nc.sbuf_tensor(name, shape, dt))

        def sem(name):
            return ctx.enter_context(nc.semaphore(name))

        xT = sb("xT", [P, KT, T])
        hT = sb("hT", [P, KT, T])
        ynT = hT
        grid = sb("grid", [P, KEYS * T])
        ring = sb("ring", [P, RING, BLOCK])
        K = sb("K", [P, N_CONST])
        S = sb("S", [P, DEPTH, N_SMALL])
        V = sb("V", [P, N_VEC])
        t5 = sb("t5", [P, HEADS, P + T])
        rope = sb("rope", [P, 3, T])
        stage = sb("stage", [P, 2048])
        pick = sb("pick", [P, 3, T])
        mod = sb("mod", [P, ADA])
        tiny = sb("tiny", [P, 256])

        def g(at, *shape):
            n = int(np.prod(shape))
            v = grid[:, at:at + n]
            if len(shape) == 2:
                v = v.rearrange("p (a b) -> p a b", a=shape[0])
            if len(shape) == 3:
                v = v.rearrange("p (a b c) -> p a b c", a=shape[0], b=shape[1])
            return v

        du = g(0, 2, T)
        iq = g(512, 2, T)
        ik = g(1024, T)
        aq = g(1280, 2, T)
        ak = g(1792, 2, T)
        av = g(2304, TT, GW)
        cq = g(2816, 2, T)
        ckv = g(3328, T)
        krA = g(3584, T)
        krB = g(3840, T)
        fq = g(4096, 2, T)
        fk = g(4608, 2, T)
        fv = g(5120, TT, GW)
        iwcf = g(5632, TT, 8)
        sq = g(5696, KT, T)
        soft = g(5696, 2, HEADS, T)
        phase = g(8192, NS5 * T)
        tmp = g(10240, NS5 * T)
        cosT = g(12288, NS5 * T)
        sinT = g(14336, NS5 * T)
        vre = g(16384, NS5 * T)
        vim = g(18432, NS5 * T)
        zre = g(20480, NS5 * T)
        zim = g(22528, NS5 * T)
        y5 = g(8192, 2, T)
        g5 = g(8704, 2, T)
        sg5 = g(9216, 2, T)
        o5 = g(9728, 2, T)
        rot = g(10240, 1024)
        sqB = g(11264, 3, T)
        cqn = g(24576, 2, T)
        ckvn = g(25088, T)
        qB = g(25344, HEADS, T)
        kB = g(26368, HEADS, T)
        vB = g(27392, TT, GW)
        mA = g(27904, HEADS, P + T)
        mC = g(29440, HEADS, P + T)
        score = g(30976, T)
        work = g(31232, T)
        rstd = g(31488, T)
        rstdB = g(31744, 2, T)
        nlogf = g(8192, TT, HEADS, P)
        yrow = stage[:, 1024:1536].rearrange("p (a b) -> p a b", a=2)
        s5c = stage[:, 1536:2048]
        pT = stage[:, 0:1024].rearrange("p (q j t) -> p q j t", q=4, j=2)
        s5raw = sb("s5raw", [P, 1024])
        cre = s5raw[:, 0:256].rearrange("p (j c) -> p j c", j=NS5)
        cim = s5raw[:, 256:512].rearrange("p (j c) -> p j c", j=NS5)
        wglu = s5raw[:, 512:1024].rearrange("p (k o) -> p k o", k=2)
        csre = s5c[:, 0:256].rearrange("p (j c) -> p j c", j=NS5)
        csim = s5c[:, 256:512].rearrange("p (j c) -> p j c", j=NS5)
        gT4 = lambda a: grid[:, a:a + 512]

        scores = g(104 * T, 2 * PH, 2 * P)
        onehot = g(120 * T, 2048)
        qT = sq

        tpos = [0]

        def tn(n):
            tpos[0] += n
            return tiny[:, tpos[0] - n:tpos[0]]

        siluc = tn(KT)
        sc1 = tn(KT)
        sc2 = tn(KT)
        dt5, lr5, th5, mag5, phi5, phh5, phl5, ta5, tb5, tc5, cre5, cim5 = [tn(NS5) for _ in range(12)]
        zf = tn(TT * HEADS)
        mnf = tn(TT * HEADS)
        azf = tn(TT * HEADS)
        lf = tn(TT * HEADS)
        logf = tn(TT * HEADS)
        cumf = tn(TT * HEADS)
        nmx = tn(2 * HEADS)
        sums = tn(2 * HEADS)
        rs = tn(2 * HEADS)
        yss = tn(2)
        yrs = tn(2)
        v8 = tn(8)
        posc = tn(2)
        epst = tn(1)
        zero = tn(1)
        drel = sb("drel", [P, (BUCKETS - 1) * HEADS])
        wk = sb("wk", [P, 256])
        vals = sb("vals", [P, PH, 2, PK])
        idxu = sb("idxu", [P, PH, 2, PK], U32)
        vc = sb("vc", [P, TT, PH, PK])
        icu = sb("icu", [P, PH, PK], U32)
        idxf = sb("idxf", [P, PH, 2, PK])
        icf = sb("icf", [P, 2, PH, PK])
        res = sb("res", [P, TT, 3, P])
        zeros = sb("zeros", [P, P])
        icu2 = sb("icu2", [P, PH, PK], U32)
        gsum = tn(PH)
        posi = grid[:, 4096:4096 + T + TT].bitcast(I32)
        posf = g(0, T)
        ang = g(512, 3, T)
        kk = g(1536, 3, T)
        kw = g(2560, 3, T)
        dist = g(5120, P + T)
        ge = g(5632, P + T)

        def const(name):
            return K[:, CONST_AT[name][0]:CONST_AT[name][1]]

        def small_of(l, name):
            return S[:, l, SMALL_AT[name][0]:SMALL_AT[name][1]]

        ident, ones, iota = const("ident"), const("ones"), const("iota")
        utri = const("utri").rearrange("p (j t) -> p j t", j=TT)
        causal = const("causal")

        bank = ctx.enter_context(nc.psum_tensor("bank", [P, 8, 512], F32))

        def region(p):
            return bank[:, p % 2, 0:T]

        def pair(w):
            return bank[:, 2 + 2 * w:4 + 2 * w, :].rearrange("p b c -> p (b c)")

        def turned(w):
            return pair(w).rearrange("p (q j t) -> p q j t", q=HEADS, j=TT)

        const_in, small_in, vec_in, pos_in, x_loaded = (sem(n) for n in ("const_in", "small_in", "vec_in", "pos_in", "x_loaded"))
        slot_filled = [sem(f"slot_filled{i}") for i in range(RING)]
        block_used = sem("block_used")
        s5w_in = sem("s5w_in")
        silu_ready = sem("silu_ready")
        mod_sums, mod_ready = sem("mod_sums"), sem("mod_ready")
        region_filled, act_taken, dve_taken = sem("region_filled"), sem("act_taken"), sem("dve_taken")
        sq_ready, root_ready, xr_ready, h_ready = sem("sq_ready"), sem("root_ready"), sem("xr_ready"), sem("h_ready")
        rope_arg, rope_sin, rope_ready = sem("rope_arg"), sem("rope_sin"), sem("rope_ready")
        s5_exp, s5_lr, s5_mag, trig_arg, trig_ready, trig_arg2 = (sem(n) for n in ("s5_exp", "s5_lr", "s5_mag", "trig_arg", "trig_ready", "trig_arg2"))
        bu_ready, bu_taken, x5_ready = sem("bu_ready"), sem("bu_taken"), sem("x5_ready")
        y5_ready, g5_ready, sig_ready, sq5_ready, o5_sq = (sem(n) for n in ("y5_ready", "g5_ready", "sig_ready", "sq5_ready", "o5_sq"))
        sqB_ready, latent_ready, qB_ready = sem("sqB_ready"), sem("latent_ready"), sem("qB_ready")
        f_abs, f_exp, f_log, logf_ready, cb_ready, mc_ready = (sem(n) for n in ("f_abs", "f_exp", "f_log", "logf_ready", "cb_ready", "mc_ready"))
        dots_ready, relu_ready, score_ready = sem("dots_ready"), sem("relu_ready"), sem("score_ready")
        logits_ready, logits_taken, max_ready, probs_ready = (sem(n) for n in ("logits_ready", "logits_taken", "max_ready", "probs_ready"))
        pt_ready, pt_taken, pv_done, pv_taken = sem("pt_ready"), sem("pt_taken"), sem("pv_done"), sem("pv_taken")
        yss_ready, yrs_ready, yn_ready = sem("yss_ready"), sem("yrs_ready"), sem("yn_ready")
        x_mixed = sem("x_mixed")
        kr_ready = sem("kr_ready")
        gate_max, gate_exp, picked, pick_ready = sem("gate_max"), sem("gate_exp"), sem("picked"), sem("pick_ready")
        a_ready, gelu_done = sem("a_ready"), sem("gelu_done")
        hot_ready, hot_used, g_ready, w_ready = sem("hot_ready"), sem("hot_used"), sem("g_ready"), sem("w_ready")
        y_ready, x_done = sem("y_ready"), sem("x_done")
        out_ready, out_stored = sem("out_ready"), sem("out_stored")
        dve_step, act_step, pool_step, zero_ready = sem("dve_step"), sem("act_step"), sem("pool_step"), sem("zero_ready")

        hotA = stage[:, 0:1024].rearrange("p (s a) -> p s a", s=8)
        hotB = stage[:, 1024:2048].rearrange("p (s a) -> p s a", s=8)

        block = ctx.enter_context(nc.Block())

        def table_at(l):
            return l * LAYER_BLOCKS + LAYER_BLOCKS - 2 * KEYS

        @block.sync
        def _(sp):
            sp.dma_start(K[:, :], consts).then_inc(const_in, 16)
            sp.dma_start(V[:, :], vec).then_inc(vec_in, 16)
            sp.dma_start(S[:, :, :], small).then_inc(small_in, 16)
            for s in range(RING):
                sp.dma_start(ring[:, s, :], stream[s]).then_inc(slot_filled[s], 16)
                if s == 0:
                    sp.dma_start(posi, pos).then_inc(pos_in, 16)
                    sp.dma_start(xT[:, :, :], x_in).then_inc(x_loaded, 16)
            turns = (N_BLOCKS - RING) // RING
            with sp.Fori(0, turns, 1) as i:
                for s in range(RING):
                    sp.wait_ge(block_used, i * RING + s + 1)
                    sp.dma_start(ring[:, s, :], stream[bass.ds(i * RING + RING + s, 1)].rearrange("o p c -> (o p) c"))\
                        .then_inc(slot_filled[s], 16)
            for n in range(RING * (turns + 1), N_BLOCKS):
                sp.wait_ge(block_used, n - RING + 1)
                sp.dma_start(ring[:, n % RING, :], stream[n]).then_inc(slot_filled[n % RING], 16)
            sp.wait_ge(out_ready, 1)
            sp.dma_start(out, hT[:, :, :]).then_inc(out_stored, 16)
            sp.wait_ge(out_stored, 16)

        @block.gpsimd
        def _(pool):
            for l in range(DEPTH):
                pool.wait_ge(const_in, 16)
                for n in range(6):
                    pool.wait_ge(yss_ready, 6 * l + n + 1)
                    nc.gpsimd.tensor_tensor(yrs[:, n % 2:n % 2 + 1], yss[:, n % 2:n % 2 + 1], const("neghalf")[:, 0:1],
                                            ALU.pow).then_inc(yrs_ready, 1)

        def out_rows(act, l, n, take):
            grp, i = n // 2, n % 2
            kt0 = [4, 2, 0][grp]
            if n == 0:
                act.wait_ge(region_filled, l * N_REG + REG_POS["fv1"] + 1)
            t = take(l, f"yt{n}")
            for k in range(2):
                last = nc.scalar.activation(ynT[:, kt0 + k, i * P:i * P + P], t[:, k * P:k * P + P], ACT.Copy,
                                            scale=small_of(l, "gng")[:, kt0 + k:kt0 + k + 1])
            last.then_inc(act_taken, 1)

        @block.scalar
        def _(act):
            steps = [0]

            def link(ins):
                steps[0] += 1
                ins.then_inc(act_step, 1)
                act.wait_ge(act_step, steps[0])

            def take(l, name):
                p = l * N_REG + REG_POS[name]
                act.wait_ge(region_filled, p + 1)
                return region(p)

            def copy(l, name, dst, scale=1.0):
                return nc.scalar.activation(dst, take(l, name)[:, 0:dst.free_size()], ACT.Copy, scale=scale)\
                    .then_inc(act_taken, 1)

            def root(l, name, n, dst):
                nc.scalar.activation(dst, take(l, name), ACT.Sqrt, bias=epst[:, 0:1], scale=1.0 / n).then_inc(act_taken, 1)

            act.wait_ge(vec_in, 16)
            act.wait_ge(zero_ready, 1)
            nc.scalar.activation(siluc[:, :], V[:, VEC_AT["c"][0]:VEC_AT["c"][1]], ACT.Sigmoid).then_inc(silu_ready, 1)
            act.wait_ge(rope_arg, 1)
            nc.scalar.activation(rope[:, :, :], kw, ACT.Sin).then_inc(rope_sin, 1)
            for l in range(DEPTH):
                act.wait_ge(small_in, 16)
                if l:
                    act.wait_ge(x_done, l)
                act.dma_start(s5raw[:, :], s5w[l]).then_inc(s5w_in, 16)
                nc.scalar.activation(dt5, small_of(l, "ldt"), ACT.Exp).then_inc(s5_exp, 1)
                act.wait_ge(s5_lr, l + 1)
                nc.scalar.activation(mag5, lr5, ACT.Exp).then_inc(s5_mag, 1)
                act.wait_ge(trig_arg, l + 1)
                nc.scalar.activation(sinT, phase, ACT.Sin, scale=TWOPI).then_inc(trig_ready, 1)
                act.wait_ge(trig_arg2, l + 1)
                nc.scalar.activation(cosT, tmp, ACT.Sin, scale=-TWOPI).then_inc(trig_ready, 1)
                act.wait_ge(x_loaded, 16)
                nc.scalar.activation(sq, xT[:, :, :], ACT.Square).then_inc(sq_ready, 1)
                root(l, "ss1", D, rstd)
                for k in range(KT):
                    act.wait_ge(xr_ready, 2 * KT * l + k + 1)
                    nc.scalar.activation(hT[:, k, :], sq[:, k, :], ACT.Identity, bias=mod[:, k:k + 1],
                                         scale=sc1[:, k:k + 1]).then_inc(h_ready, 1)
                for i in range(2):
                    copy(l, f"du{i}", du[:, i, :])
                for i in range(2):
                    copy(l, f"iq{i}", iq[:, i, :])
                copy(l, "ik", ik)
                for i in range(2):
                    copy(l, f"aq{i}", aq[:, i, :], HD ** -0.5)
                for i in range(2):
                    copy(l, f"ak{i}", ak[:, i, :])
                for i in range(2):
                    nc.scalar.activation(av[:, :, i * P:i * P + P], take(l, f"av{i}").rearrange("p (a b) -> p a b", a=TT),
                                         ACT.Copy).then_inc(act_taken, 1)
                copy(l, "iwcf", grid[:, 5632:5648])
                for i in range(TT):
                    w = (i + 1) * P
                    act.wait_ge(dots_ready, TT * l + i + 1)
                    nc.scalar.activation(soft[:, i, :, 0:w], pair(i).rearrange("p (q s) -> p q s", q=HEADS)[:, :, 0:w],
                                         ACT.Relu).then_inc(relu_ready, 1)
                for i in range(2):
                    copy(l, f"cq{i}", cq[:, i, :])
                copy(l, "ckv", ckv)
                link_waits = taken_count(l, "ckv")[1]
                act.wait_ge(act_taken, link_waits)
                nc.scalar.activation(sqB[:, 0:2, :], cq, ACT.Square)
                nc.scalar.activation(sqB[:, 2, :], ckv, ACT.Square).then_inc(sqB_ready, 1)
                for n, dst in (("krA", krA), ("krB", krB)):
                    nc.scalar.activation(dst[64:P], take(l, n)[64:P], ACT.Copy).then_inc(act_taken, 1)
                for i in range(2):
                    copy(l, f"fq{i}", fq[:, i, :], HD ** -0.5)
                for i in range(2):
                    copy(l, f"fk{i}", fk[:, i, :])
                for i in range(2):
                    nc.scalar.activation(fv[:, :, i * P:i * P + P], take(l, f"fv{i}").rearrange("p (a b) -> p a b", a=TT),
                                         ACT.Copy).then_inc(act_taken, 1)
                root(l, "ssq", GW, rstdB[:, 0, :])
                root(l, "sskv", KV_RANK, rstdB[:, 1, :])
                act.wait_ge(f_abs, l + 1)
                nc.scalar.activation(lf, azf, ACT.Exp, scale=-1.0).then_inc(f_exp, 1)
                act.wait_ge(f_exp, l + 1)
                nc.scalar.activation(lf, lf, ACT.Ln, bias=1.0).then_inc(f_log, 1)
                copy(l, "fcum", cumf)
                for h in range(HEADS):
                    nc.scalar.activation(kB[0:NOPE, h, :], take(l, f"kB{h}")[0:NOPE], ACT.Copy).then_inc(act_taken, 1)
                for i in range(TT):
                    copy(l, f"vB{i}", vB[:, i, :])
                for i in range(2):
                    act.wait_ge(dve_taken, taken_count(l, f"y5_{i}")[1])
                    nc.scalar.activation(g5[:, i, :], y5[:, i, :], ACT.Gelu_apprx_tanh).then_inc(g5_ready, 1)
                for i in range(2):
                    nc.scalar.activation(sg5[:, i, :], take(l, f"glu{i}"), ACT.Sigmoid, bias=small_of(l, "bglu")[:, i:i + 1])\
                        .then_inc(act_taken, 1)
                root(l, "ss5", GW, rstd)
                for n in range(6):
                    w = (n % 2 + 1) * P
                    act.wait_ge(max_ready, 6 * l + n + 1)
                    for q in range(HEADS):
                        h = PERM[q]
                        last = nc.scalar.activation(soft[:, n % 2, q, 0:w], soft[:, n % 2, q, 0:w], ACT.Exp,
                                                    bias=nmx[:, 4 * (n % 2) + q:4 * (n % 2) + q + 1],
                                                    accum_out=sums[:, 4 * (n % 2) + h:4 * (n % 2) + h + 1])
                    last.then_inc(probs_ready, 1)
                    for b in range(2):
                        act.wait_ge(pt_ready, (6 * l + n) * 2 + b + 1)
                        j = n % 2 + 1
                        nc.scalar.activation(pT[:, 2 * b:2 * b + 2, 0:j, :], turned((n + 1) % 2)[:, 2 * b:2 * b + 2, 0:j, :],
                                             ACT.Copy).then_inc(pt_taken, 1)
                    if n:
                        out_rows(act, l, n - 1, take)
                out_rows(act, l, 5, take)
                act.wait_ge(dve_taken, taken_count(l, f"out{KT - 1}")[1])
                nc.scalar.activation(sq, xT[:, :, :], ACT.Square).then_inc(sq_ready, 1)
                root(l, "ss2", D, rstd)
                for k in range(KT):
                    act.wait_ge(xr_ready, 2 * KT * l + KT + k + 1)
                    nc.scalar.activation(hT[:, k, :], sq[:, k, :], ACT.Identity, bias=mod[:, 3 * KT + k:3 * KT + k + 1],
                                         scale=sc2[:, k:k + 1]).then_inc(h_ready, 1)
                for h in range(PH):
                    for w in range(2):
                        copy(l, f"pq{h}_{w}", qT[:, 2 * (h % 2) + w, :])
                    for i in range(TT):
                        copy(l, f"sc{h}_{i}", scores[:, i * PH + h, :])
                first = KEYS // 2 * l

                def gelu(pairs, at, bank_n):
                    act.wait_ge(a_ready, pairs)
                    nc.scalar.activation(at, bank[:, bank_n, :], ACT.Gelu_apprx_tanh).then_inc(gelu_done, 1)

                def gates():
                    for i in range(TT):
                        act.wait_ge(gate_max, TT * l + i + 1)
                        nc.scalar.activation(vc[:, i, :, :], vc[:, i, :, :], ACT.Exp).then_inc(gate_exp, 1)

                lo = 8
                with act.Fori(0, lo, 1) as i:
                    for j in range(4):
                        gelu(i * 4 + (first + j + 1), grid[:, bass.ds(i * (8 * T) + j * 2 * T, 2 * T)], j)
                gates()
                with act.Fori(lo, 13, 1) as i:
                    for j in range(4):
                        gelu(i * 4 + (first + j + 1), grid[:, bass.ds(i * (8 * T) + j * 2 * T, 2 * T)], j)
                act.wait_ge(picked, TT * (l + 1))
                with act.Fori(13, 16, 1) as i:
                    for j in range(4):
                        gelu(i * 4 + (first + j + 1), grid[:, bass.ds(i * (8 * T) + j * 2 * T, 2 * T)], j)
                for i in range(TT):
                    for r in range(3):
                        nc.scalar.activation(pick[:, r, i * P:i * P + P], take(l, f"tr{3 * i + r}")[:, 0:P], ACT.Copy)\
                            .then_inc(act_taken, 1)
            act.wait_ge(x_done, DEPTH)
            nc.scalar.activation(sq, xT[:, :, :], ACT.Square).then_inc(sq_ready, 1)
            act.wait_ge(region_filled, DEPTH * N_REG + 1)
            nc.scalar.activation(rstd, bank[:, 0, 0:T], ACT.Sqrt, bias=epst[:, 0:1], scale=1.0 / D).then_inc(act_taken, 1)

        @block.vector
        def _(dve):
            v = nc.vector
            steps = [0]

            def link(ins):
                steps[0] += 1
                ins.then_inc(dve_step, 1)
                dve.wait_ge(dve_step, steps[0])

            def take(l, name):
                p = l * N_REG + REG_POS[name]
                dve.wait_ge(region_filled, p + 1)
                return region(p)

            v.memset(epst, EPS)
            v.memset(zeros[:, :], 0.0).then_inc(zero_ready, 1)
            dve.wait_ge(silu_ready, 1)
            v.tensor_tensor(siluc, siluc, V[:, VEC_AT["c"][0]:VEC_AT["c"][1]], ALU.mult).then_inc(silu_ready, 1)
            dve.wait_ge(pos_in, 16)
            dve.wait_ge(const_in, 16)
            v.tensor_copy(posf, posi[:, 0:T])
            link(v.tensor_copy(posc, posi[:, T:T + TT]))
            for i in range(3):
                last = v.tensor_scalar(ang[:, i, :], posf, const("freq")[:, i:i + 1], None, ALU.mult)
            link(last)
            link(v.tensor_scalar(kk, ang, INV2PI, MAGIC, ALU.mult, ALU.add))
            link(v.tensor_scalar(kk, kk, -MAGIC, None, ALU.add))
            link(v.scalar_tensor_tensor(ang, kk, -C1, ang, ALU.mult, ALU.add))
            link(v.scalar_tensor_tensor(ang, kk, -C2, ang, ALU.mult, ALU.add))
            link(v.scalar_tensor_tensor(ang, kk, -C3, ang, ALU.mult, ALU.add))
            for i in range(3):
                last = v.tensor_scalar(kk[:, i, :], ang[:, i, :], const("phase")[:, i:i + 1], None, ALU.add)
            link(last)
            link(v.tensor_scalar(kw, kk, PI, -2 * PI, ALU.is_gt, ALU.mult))
            link(v.tensor_tensor(kw, kw, kk, ALU.add))
            v.tensor_scalar(kw, kw, PI, -PI, ALU.min, ALU.max).then_inc(rope_arg, 1)
            r0 = VEC_AT["rel"][0]
            dve.wait_ge(vec_in, 16)
            link(v.tensor_tensor(drel[:, :], V[:, r0 + HEADS:r0 + BUCKETS * HEADS], V[:, r0:r0 + (BUCKETS - 1) * HEADS], ALU.subtract))
            v.tensor_scalar(dist[:, 0:P], posf[:, 0:P], posc[:, 0:1], -1.0, ALU.subtract, ALU.mult)
            link(v.tensor_scalar(dist[:, P:P + T], posf, posc[:, 1:2], -1.0, ALU.subtract, ALU.mult))
            for q in range(HEADS):
                h = PERM[q]
                last = v.tensor_scalar(t5[:, q, :], dist, 0.0, V[:, r0 + h:r0 + h + 1], ALU.mult, ALU.add)
            link(last)
            base = steps[0]
            with dve.Fori(0, BUCKETS - 1, 1) as b:
                v.tensor_scalar(ge, dist, K[:, bass.ds(b + CONST_AT["thr"][0], 1)], None, ALU.is_ge).then_inc(dve_step, 1)
                dve.wait_ge(dve_step, b * 2 + (base + 1))
                for q in range(HEADS):
                    h = PERM[q]
                    last = v.scalar_tensor_tensor(t5[:, q, :], ge, drel[:, bass.ds(b * HEADS + h, 1)], t5[:, q, :], ALU.mult, ALU.add)
                last.then_inc(dve_step, 1)
                dve.wait_ge(dve_step, b * 2 + (base + 2))
            steps[0] += 2 * (BUCKETS - 1)
            dve.wait_ge(rope_sin, 1)
            for i in range(3):
                last = v.tensor_scalar(rope[:, i, :], rope[:, i, :], const("mul")[:, i:i + 1], None, ALU.mult)
            link(last)
            for l in range(DEPTH):
                sm = lambda n: small_of(l, n)
                dve.wait_ge(small_in, 16)
                dve.wait_ge(s5_exp, l + 1)
                v.tensor_tensor(lr5, sm("lre"), dt5, ALU.mult).then_inc(s5_lr, 1)
                link(v.tensor_tensor(th5, sm("lim"), dt5, ALU.mult))
                link(v.tensor_scalar(phi5, th5, INV2PI, None, ALU.mult))
                link(v.tensor_scalar(ta5, phi5, 4097.0, None, ALU.mult))
                link(v.tensor_tensor(tb5, ta5, phi5, ALU.subtract))
                link(v.tensor_tensor(phh5, ta5, tb5, ALU.subtract))
                link(v.tensor_tensor(phl5, phi5, phh5, ALU.subtract))
                ph3 = phase.rearrange("p (j t) -> p j t", j=NS5)
                tm3 = tmp.rearrange("p (j t) -> p j t", j=NS5)
                time = const("time").unsqueeze(1).broadcast_to([P, NS5, T])
                link(v.tensor_tensor(ph3, time, phh5.unsqueeze(2).broadcast_to([P, NS5, T]), ALU.mult))
                link(v.tensor_scalar(tmp, phase, MAGIC, -MAGIC, ALU.add, ALU.add))
                link(v.tensor_tensor(phase, phase, tmp, ALU.subtract))
                link(v.tensor_tensor(tm3, time, phl5.unsqueeze(2).broadcast_to([P, NS5, T]), ALU.mult))
                link(v.tensor_tensor(phase, phase, tmp, ALU.add))
                link(v.tensor_scalar(tmp, phase, MAGIC, -MAGIC, ALU.add, ALU.add))
                v.tensor_tensor(phase, phase, tmp, ALU.subtract).then_inc(trig_arg, 1)
                dve.wait_ge(trig_arg, l + 1)
                link(v.tensor_scalar(tmp, phase, 0.25, None, ALU.add))
                v.scalar_tensor_tensor(tmp, tmp, 0.5, tmp, ALU.is_gt, ALU.subtract).then_inc(trig_arg2, 1)
                dve.wait_ge(block_used, l * LAYER_BLOCKS + ADA)
                link(v.tensor_tensor(mod[:, :], bank[:, 7, 0:ADA], sm("adab"), ALU.add))
                v.scalar_tensor_tensor(sc1, mod[:, KT:2 * KT], 1.0, sm("n1g"), ALU.add, ALU.mult)
                link(v.scalar_tensor_tensor(sc2, mod[:, 4 * KT:5 * KT], 1.0, sm("n2g"), ALU.add, ALU.mult))

                def normed(l, which):
                    dve.wait_ge(act_taken, taken_count(l, which)[1])
                    link(v.reciprocal(rstd, rstd))
                    for k in range(KT):
                        v.tensor_tensor(sq[:, k, :], xT[:, k, :], rstd, ALU.mult).then_inc(xr_ready, 1)

                normed(l, "ss1")
                dve.wait_ge(trig_ready, 2 * (l + 1))
                dve.wait_ge(s5_mag, l + 1)
                c3 = cosT.rearrange("p (j t) -> p j t", j=NS5)
                s3 = sinT.rearrange("p (j t) -> p j t", j=NS5)
                v.tensor_tensor(ta5, mag5, c3[:, :, 1], ALU.mult)
                link(v.tensor_tensor(tb5, mag5, s3[:, :, 1], ALU.mult))
                link(v.tensor_scalar(ta5, ta5, -1.0, None, ALU.add))
                v.tensor_tensor(cre5, ta5, sm("lre"), ALU.mult)
                v.tensor_tensor(tc5, tb5, sm("lim"), ALU.mult)
                v.tensor_tensor(cim5, tb5, sm("lre"), ALU.mult)
                link(v.tensor_tensor(phi5, ta5, sm("lim"), ALU.mult))
                v.tensor_tensor(cre5, cre5, tc5, ALU.add)
                link(v.tensor_tensor(cim5, cim5, phi5, ALU.subtract))
                v.tensor_tensor(ta5, sm("lre"), sm("lre"), ALU.mult)
                link(v.tensor_tensor(tb5, sm("lim"), sm("lim"), ALU.mult))
                link(v.tensor_tensor(ta5, ta5, tb5, ALU.add))
                link(v.reciprocal(ta5, ta5))
                v.tensor_tensor(cre5, cre5, ta5, ALU.mult)
                link(v.tensor_tensor(cim5, cim5, ta5, ALU.mult))
                dve.wait_ge(s5w_in, 16 * (l + 1))
                crb = cre5.unsqueeze(2).broadcast_to([P, NS5, C5])
                cib = cim5.unsqueeze(2).broadcast_to([P, NS5, C5])
                s5t = wk[:, :].rearrange("p (j c) -> p j c", j=NS5)
                v.tensor_tensor(csre, cre, crb, ALU.mult)
                link(v.tensor_tensor(s5t, cim, cib, ALU.mult))
                link(v.tensor_tensor(csre, csre, s5t, ALU.subtract))
                v.tensor_tensor(csim, cre, cib, ALU.mult)
                link(v.tensor_tensor(s5t, cim, crb, ALU.mult))
                link(v.scalar_tensor_tensor(csim, csim, -1.0, s5t, ALU.mult, ALU.subtract))
                for m in range(2):
                    dve.wait_ge(bu_ready, 2 * l + m + 1)
                    s = slice(1024 * m, 1024 * m + 1024)
                    br, bi = pair(0), pair(1)
                    v.tensor_tensor(vre[:, s], cosT[:, s], br, ALU.mult)
                    link(v.tensor_tensor(rot, sinT[:, s], bi, ALU.mult))
                    v.tensor_tensor(vre[:, s], vre[:, s], rot, ALU.add)
                    link(v.tensor_tensor(vim[:, s], cosT[:, s], bi, ALU.mult))
                    v.tensor_tensor(rot, sinT[:, s], br, ALU.mult).then_inc(bu_taken, 1)
                    dve.wait_ge(bu_taken, 2 * l + m + 1)
                    link(v.tensor_tensor(vim[:, s], vim[:, s], rot, ALU.subtract))
                for j in range(NS5):
                    s = slice(T * j, T * j + T)
                    m = mag5[:, j:j + 1].broadcast_to([P, T])
                    v.tensor_tensor_scan(zre[:, s], m, vre[:, s], 0.0, ALU.mult, ALU.add)
                    last = v.tensor_tensor_scan(zim[:, s], m, vim[:, s], 0.0, ALU.mult, ALU.add)
                link(last)
                v.tensor_tensor(vre, cosT, zre, ALU.mult)
                link(v.tensor_tensor(phase, sinT, zim, ALU.mult))
                link(v.tensor_tensor(vre, vre, phase, ALU.subtract))
                v.tensor_tensor(vim, cosT, zim, ALU.mult)
                link(v.tensor_tensor(phase, sinT, zre, ALU.mult))
                v.tensor_tensor(vim, vim, phase, ALU.add).then_inc(x5_ready, 1)
                dve.wait_ge(x5_ready, l + 1)
                dve.wait_ge(act_taken, taken_count(l, "iwcf")[1])
                z3 = zf.rearrange("p (i h) -> p i h", i=TT)
                link(v.tensor_tensor(z3, iwcf[:, :, HEADS:8], sm("bf").unsqueeze(1).broadcast_to([P, TT, HEADS]), ALU.add))
                link(v.tensor_scalar(mnf, zf, 0.0, None, ALU.min))
                link(v.tensor_scalar(azf, zf, -1.0, None, ALU.mult))
                v.tensor_tensor(azf, zf, azf, ALU.max).then_inc(f_abs, 1)
                for i in range(TT):
                    w = (i + 1) * P
                    at = 0 if i == 0 else P
                    dve.wait_ge(relu_ready, TT * l + i + 1)
                    link(v.tensor_scalar(score[:, 0:w], soft[:, i, 0, 0:w], iwcf[:, i, 0:1], None, ALU.mult))
                    for q in range(1, HEADS):
                        h = PERM[q]
                        link(v.scalar_tensor_tensor(score[:, 0:w], soft[:, i, q, 0:w], iwcf[:, i, h:h + 1], score[:, 0:w],
                                                    ALU.mult, ALU.add))
                    link(v.tensor_tensor(work[:, 0:w], score[:, 0:w], causal[:, at:at + w], ALU.add))
                    for _ in range(TOPK // 8):
                        link(v.max(v8, work[:, 0:w]))
                        link(v.match_replace(work[:, 0:w], v8, work[:, 0:w], TAKEN))
                    link(v.tensor_scalar(work[:, 0:w], work[:, 0:w], TAKEN / 2, -BIG, ALU.is_ge, ALU.mult))
                    link(v.tensor_tensor(work[:, 0:w], work[:, 0:w], causal[:, at:at + w], ALU.add))
                    link(v.tensor_tensor(mA[:, :, at:at + w], t5[:, :, at:at + w],
                                         work[:, 0:w].unsqueeze(1).broadcast_to([P, HEADS, w]), ALU.add))
                dve.wait_ge(act_taken, taken_count(l, "sskv")[1])
                link(v.reciprocal(rstdB, rstdB))
                for i in range(2):
                    v.scalar_tensor_tensor(cqn[:, i, :], cq[:, i, :], sm("qg")[:, i:i + 1], rstdB[:, 0, :], ALU.mult, ALU.mult)
                v.scalar_tensor_tensor(ckvn, ckv, sm("kvg")[:, 0:1], rstdB[:, 1, :], ALU.mult, ALU.mult)\
                    .then_inc(latent_ready, 1)
                hi = slice(64, P)
                v.tensor_tensor(krA[hi], krA[hi], rope[hi, 1, :], ALU.mult)
                link(v.tensor_tensor(krB[hi], krB[hi], rope[hi, 2, :], ALU.mult))
                link(v.tensor_tensor(krA[hi], krA[hi], krB[hi], ALU.add))
                v.tensor_copy(kB[hi, :, :], krA[hi].unsqueeze(1).broadcast_to([64, HEADS, T])).then_inc(kr_ready, 1)
                dve.wait_ge(f_log, l + 1)
                v.tensor_tensor(logf, mnf, lf, ALU.subtract)
                link(v.tensor_tensor(azf, lf, mnf, ALU.subtract))
                for i in range(TT):
                    last = v.tensor_copy(nlogf[:, i, :, :], azf[:, i * HEADS:i * HEADS + HEADS].unsqueeze(2)
                                         .broadcast_to([P, HEADS, P]))
                last.then_inc(logf_ready, 1)
                for h in range(HEADS):
                    v.tensor_tensor(qB[:, h, :], take(l, f"qB{h}"), rope[:, 0, :], ALU.mult).then_inc(dve_taken, 1)
                dve.wait_ge(cb_ready, l + 1)
                dve.wait_ge(act_taken, taken_count(l, "fcum")[1])
                for i in range(TT):
                    w = (i + 1) * P
                    at = 0 if i == 0 else P
                    for q in range(HEADS):
                        h = PERM[q]
                        last = v.scalar_tensor_tensor(mC[:, q, at:at + w], pair(0)[:, h * T:h * T + w],
                                                      cumf[:, i * HEADS + h:i * HEADS + h + 1], causal[:, at:at + w],
                                                      ALU.add, ALU.add)
                last.then_inc(mc_ready, 1)
                for i in range(2):
                    v.scalar_tensor_tensor(y5[:, i, :], du[:, i, :], sm("D")[:, i:i + 1], take(l, f"y5_{i}"), ALU.mult, ALU.add)\
                        .then_inc(dve_taken, 1)
                dve.wait_ge(act_taken, taken_count(l, "glu1")[1])
                link(v.tensor_tensor(o5, g5, sg5, ALU.mult))
                v.tensor_tensor(sg5, o5, o5, ALU.mult).then_inc(sq5_ready, 1)
                dve.wait_ge(act_taken, taken_count(l, "ss5")[1])
                link(v.reciprocal(rstd, rstd))
                for i in range(2):
                    last = v.scalar_tensor_tensor(ynT[:, 6 + i, :], o5[:, i, :], sm("gng")[:, 6 + i:7 + i], rstd, ALU.mult, ALU.mult)
                link(last)

                def maxima(n):
                    grp, i = n // 2, n % 2
                    w = (i + 1) * P
                    at = 0 if i == 0 else P
                    u = 6 * l + n
                    dve.wait_ge(logits_ready, u + 1)
                    if n == 0:
                        dve.wait_ge(mc_ready, l + 1)
                    m = [mC[:, :, at:at + w], causal[:, at:at + w].unsqueeze(1).broadcast_to([P, HEADS, w]),
                         mA[:, :, at:at + w]][grp]
                    if n >= 2:
                        dve.wait_ge(pt_ready, (u - 1) * 2)
                    v.tensor_tensor(soft[:, i, :, 0:w], pair((n + 1) % 2).rearrange("p (q s) -> p q s", q=HEADS)[:, :, 0:w],
                                    m, ALU.add).then_inc(logits_taken, 1)
                    dve.wait_ge(logits_taken, u + 1)
                    v.tensor_reduce(nmx[:, 4 * i:4 * i + 4], soft[:, i, :, 0:w], AX_X, ALU.max, negate=True)\
                        .then_inc(max_ready, 1)

                def outputs(n):
                    i = n % 2
                    u = 6 * l + n
                    dve.wait_ge(probs_ready, u + 1)
                    link(v.reciprocal(rs[:, 4 * i:4 * i + 4], sums[:, 4 * i:4 * i + 4]))
                    dve.wait_ge(pv_done, u + 1)
                    y3 = yrow[:, i, :].rearrange("p (h d) -> p h d", h=HEADS)
                    if n >= 2:
                        dve.wait_ge(region_filled, l * N_REG + REG_POS[f"yt{n - 2}"] + 1)
                    v.tensor_tensor(y3, bank[:, 6 + i, 0:GW].rearrange("p (h d) -> p h d", h=HEADS),
                                    rs[:, 4 * i:4 * i + 4].unsqueeze(2).broadcast_to([P, HEADS, HD]), ALU.mult)\
                        .then_inc(pv_taken, 1)
                    dve.wait_ge(pv_taken, u + 1)
                    v.tensor_tensor_reduce(wk[:, 0:GW], yrow[:, i, :], yrow[:, i, :], 1.0 / GW, EPS, ALU.mult, ALU.add,
                                           yss[:, i:i + 1]).then_inc(yss_ready, 1)
                    dve.wait_ge(yrs_ready, u + 1)
                    v.tensor_scalar(yrow[:, i, :], yrow[:, i, :], yrs[:, i:i + 1], None, ALU.mult).then_inc(yn_ready, 1)

                for n in range(6):
                    maxima(n)
                    if n:
                        outputs(n - 1)
                outputs(5)
                for m in range(KT):
                    v.scalar_tensor_tensor(xT[:, m, :], take(l, f"out{m}"), mod[:, 2 * KT + m:2 * KT + m + 1], xT[:, m, :],
                                           ALU.mult, ALU.add).then_inc(dve_taken, 1)
                dve.wait_ge(dve_taken, taken_count(l, f"out{KT - 1}")[1])
                normed(l, "ss2")
                for i in range(TT):
                    for h in range(PH):
                        if i == 0:
                            dve.wait_ge(act_taken, taken_count(l, f"sc{h}_1")[1])
                        for w in range(2):
                            s = scores[:, i * PH + h, w * P:w * P + P]
                            vv, ii = vals[:, h, w, :], idxu[:, h, w, :]
                            link(v.max(vv[:, 0:8], s))
                            v.max_index(ii[:, 0:8], vv[:, 0:8], s)
                            link(v.match_replace(wk[:, 0:P], vv[:, 0:8], s, TAKEN))
                            link(v.max(vv[:, 8:16], wk[:, 0:P]))
                            link(v.max_index(ii[:, 8:16], vv[:, 8:16], wk[:, 0:P]))
                        cand = wk[:, 0:PK * PK]
                        link(v.tensor_tensor(cand.rearrange("p (i j) -> p i j", i=PK),
                                             vals[:, h, 0, :].unsqueeze(2).broadcast_to([P, PK, PK]),
                                             vals[:, h, 1, :].unsqueeze(1).broadcast_to([P, PK, PK]), ALU.add))
                        link(v.max(vc[:, i, h, 0:8], cand))
                        link(v.max_index(icu[:, h, 0:8], vc[:, i, h, 0:8], cand))
                        link(v.match_replace(cand, vc[:, i, h, 0:8], cand, TAKEN))
                        link(v.max(vc[:, i, h, 8:16], cand))
                        link(v.max_index(icu[:, h, 8:16], vc[:, i, h, 8:16], cand))
                    v.tensor_copy(gsum, vc[:, i, :, 0])
                    v.tensor_copy(idxf[:, :, :, :], idxu[:, :, :, :])
                    link(v.tensor_scalar(icu2[:, :, :], icu[:, :, :], 4, None, ALU.logical_shift_right))
                    link(v.tensor_copy(icf[:, 0, :, :], icu2[:, :, :]))
                    link(v.tensor_scalar(icu2[:, :, :], icu[:, :, :], PK - 1, None, ALU.bitwise_and))
                    link(v.tensor_copy(icf[:, 1, :, :], icu2[:, :, :]))
                    v.tensor_tensor(vc[:, i, :, :], vc[:, i, :, :], gsum.unsqueeze(2).broadcast_to([P, PH, PK]), ALU.subtract)\
                        .then_inc(gate_max, 1)
                    hot = onehot.rearrange("p (h k j) -> p h k j", h=PH, k=PK)
                    hot3 = onehot.rearrange("p (n j) -> p n j", j=PK)
                    for w in range(2):
                        link(v.tensor_tensor(hot3, icf[:, w, :, :].rearrange("p h k -> p (h k)").unsqueeze(2).broadcast_to([P, P, PK]),
                                             iota[:, 0:PK].unsqueeze(1).broadcast_to([P, P, PK]), ALU.is_equal))
                        for h in range(PH):
                            last = v.tensor_tensor(hot[:, h, :, :], hot[:, h, :, :],
                                                   idxf[:, h, w, :].unsqueeze(1).broadcast_to([P, PK, PK]), ALU.mult)
                        link(last)
                        link(v.tensor_reduce(res[:, i, w, :], hot3, AX_X, ALU.add))
                for i in range(TT):
                    dve.wait_ge(gate_exp, TT * l + i + 1)
                    link(v.tensor_reduce(gsum, vc[:, i, :, :], AX_X, ALU.add))
                    link(v.reciprocal(gsum, gsum))
                    v.tensor_tensor(res[:, i, 2, :].rearrange("p (h k) -> p h k", h=PH), vc[:, i, :, :],
                                    gsum.unsqueeze(2).broadcast_to([P, PH, PK]), ALU.mult).then_inc(picked, 1)
                    dve.wait_ge(picked, TT * l + i + 1)
                dve.wait_ge(act_taken, taken_count(l, f"tr{3 * TT - 1}")[1])
                dve.wait_ge(gelu_done, KEYS // 2 * (l + 1))
                g3 = grid[:, :].rearrange("p (a t) -> p a t", a=KEYS)

                def hots(t, half):
                    for j in range(4):
                        s = 4 * half + j
                        v.tensor_scalar(hotB[:, s, :], iota, pick[:, 1, bass.ds(t + j, 1)], None, ALU.is_equal)
                        last = v.tensor_scalar(hotA[:, s, :], iota, pick[:, 0, bass.ds(t + j, 1)],
                                               pick[:, 2, bass.ds(t + j, 1)], ALU.is_equal, ALU.mult)
                    last.then_inc(hot_ready, 1)

                def weigh(t, b):
                    gw = g3[:, :, bass.ds(t, 4)]
                    v.tensor_tensor(gw, gw, bank[:, b, :].rearrange("p (t a) -> p a t", t=4), ALU.mult).then_inc(w_ready, 1)

                quads = T // 4
                q0 = quads * l
                hots(0, 0)
                hots(4, 1)
                with dve.Fori(0, (quads - 4) // 4, 1) as i:
                    for j in range(4):
                        dve.wait_ge(g_ready, i * 4 + (q0 + j + 1))
                        weigh(i * 16 + 4 * j, j)
                        hots(i * 16 + (4 * j + 8), j % 2)
                for n in range(quads - 4, quads):
                    dve.wait_ge(g_ready, q0 + n + 1)
                    weigh(4 * n, n % 4)
                    if n + 2 < quads:
                        hots(4 * n + 8, n % 2)
                dve.wait_ge(block_used, (l + 1) * LAYER_BLOCKS)
                for m in range(KT):
                    last = v.scalar_tensor_tensor(xT[:, m, :], bank[:, 4 + m // 2, (m % 2) * T:(m % 2) * T + T],
                                                  mod[:, 5 * KT + m:5 * KT + m + 1], xT[:, m, :], ALU.mult, ALU.add)
                last.then_inc(x_done, 1)
                dve.wait_ge(x_done, l + 1)
            dve.wait_ge(act_taken, DEPTH * PER_TAKER["act"] + 1)
            link(v.reciprocal(rstd, rstd))
            f0 = VEC_AT["fg"][0]
            for m in range(KT):
                last = v.scalar_tensor_tensor(hT[:, m, :], xT[:, m, :], V[:, f0 + m:f0 + m + 1], rstd, ALU.mult, ALU.mult)
            last.then_inc(out_ready, 1)

        @block.tensor
        def _(pe):
            mm = nc.tensor.matmul
            n_block = [0]
            to_free = [0]

            def free_block(first):
                if to_free[0]:
                    first.then_inc(block_used, to_free[0])
                    to_free[0] = 0

            def load():
                n = n_block[0]
                n_block[0] += 1
                pe.wait_ge(slot_filled[n % RING], 16 * (n // RING + 1))
                return ring[:, n % RING, :].rearrange("p (k c) -> p k c", k=KT)

            def free_region(l, name):
                p = l * N_REG + REG_POS[name]
                if p >= 2:
                    w, c = taken_count((p - 2) // N_REG, REGIONS[(p - 2) % N_REG][0])
                    pe.wait_ge(act_taken if w == "act" else dve_taken, c)
                return region(p)

            def project(l, name, rhs, cols=slice(0, P), rows=slice(0, P)):
                b = load()
                r = free_region(l, name)
                for k in range(KT):
                    last = mm(r[:, :], b[:, k, :], rhs[:, k, :], start=(k == 0), stop=(k == KT - 1))
                return last

            def sums_of(l, name, src, n):
                r = free_region(l, name)
                for k in range(n):
                    last = mm(r, ones, src[:, k, :], start=(k == 0), stop=(k == n - 1))
                    if k == 0 and n > 1:
                        free_block(last)
                last.then_inc(region_filled, 1)

            pe.wait_ge(silu_ready, 2)
            pe.wait_ge(zero_ready, 1)
            for l in range(DEPTH):
                if l:
                    pe.wait_ge(x_done, l)
                for m in range(ADA):
                    b = load()
                    for k in range(KT):
                        last = mm(bank[:, 7, m:m + 1], b[:, k, :], siluc[:, k:k + 1], start=(k == 0), stop=(k == KT - 1))
                    last.then_inc(block_used, 1)
                pe.wait_ge(const_in, 16)
                pe.wait_ge(sq_ready, 2 * l + 1)
                sums_of(l, "ss1", sq, KT)
                pe.wait_ge(h_ready, 2 * KT * l + KT)

                def transposed(name):
                    b = load()
                    r = free_region(l, name)
                    for k in range(KT):
                        last = mm(r, b[:, k, :], hT[:, k, :], start=(k == 0), stop=(k == KT - 1))
                        if k == 0:
                            free_block(last)
                    last.then_inc(region_filled, 1)
                    to_free[0] += 1

                def by_rows(name):
                    b = load()
                    r = free_region(l, name)
                    for i in range(TT):
                        for k in range(KT):
                            last = mm(r[:, i * P:i * P + P], hT[:, k, i * P:i * P + P], b[:, k, :], start=(k == 0), stop=(k == KT - 1))
                            if k == 0:
                                free_block(last)
                    last.then_inc(region_filled, 1)
                    to_free[0] += 1

                def s5_inputs(m):
                    b = load()
                    if m:
                        pe.wait_ge(bu_taken, 2 * l + m)
                    pe.wait_ge(act_taken, taken_count(l, "du1")[1])
                    for part in range(2):
                        for j in range(4):
                            last = mm(pair(part)[:, j * T:j * T + T], b[:, 4 * part + j, :], du[:, m, :], start=True, stop=True)
                            if j == 0:
                                free_block(last)
                    last.then_inc(bu_ready, 1)
                    to_free[0] += 1

                for n in ("du0", "du1", "iq0", "iq1", "ik"):
                    transposed(n)
                s5_inputs(0)
                for n in ("aq0", "aq1", "ak0", "ak1"):
                    transposed(n)
                s5_inputs(1)
                by_rows("av0")
                by_rows("av1")
                r = free_region(l, "iwcf")
                w8 = small_of(l, "iwcf").rearrange("p (k c) -> p k c", k=KT)
                pe.wait_ge(small_in, 16)
                for i in range(TT):
                    for k in range(KT):
                        last = mm(r[:, i * 8:i * 8 + 8], hT[:, k, i * P:i * P + P], w8[:, k, :], start=(k == 0), stop=(k == KT - 1))
                last.then_inc(region_filled, 1)

                def head_logits(w, i, q_of, k_of):
                    n = (i + 1) * P
                    for q in range(HEADS):
                        h = PERM[q]
                        last = mm(pair(w)[:, q * T:q * T + n], q_of(h)[:, i * P:i * P + P], k_of(h)[:, 0:n], start=True, stop=True)
                    return last

                def half(t, h):
                    lo = (h % 2) * HD
                    return t[lo:lo + HD]

                pe.wait_ge(bu_taken, 2 * (l + 1))
                pe.wait_ge(act_taken, taken_count(l, "ik")[1])
                for i in range(TT):
                    head_logits(i, i, lambda h: half(iq[:, h // 2, :], h), lambda h: half(ik, h)).then_inc(dots_ready, 1)
                for n in ("cq0", "cq1", "ckv"):
                    transposed(n)
                b = load()
                for w, name in enumerate(("krA", "krB")):
                    r = free_region(l, name)
                    for k in range(KT):
                        last = mm(r[64:P], b[:, k, 64 * w:64 * w + 64], hT[:, k, :], start=(k == 0), stop=(k == KT - 1))
                        if k == 0:
                            free_block(last)
                    last.then_inc(region_filled, 1)
                to_free[0] += 1
                for n in ("fq0", "fq1", "fk0", "fk1"):
                    transposed(n)
                by_rows("fv0")
                by_rows("fv1")
                pe.wait_ge(sqB_ready, l + 1)
                sums_of(l, "ssq", sqB, 2)
                sums_of(l, "sskv", sqB[:, 2:3, :], 1)
                pe.wait_ge(logf_ready, l + 1)
                r = free_region(l, "fcum")
                lg = logf.rearrange("p (j h) -> p j h", j=TT)
                for i in range(TT):
                    for j in range(i + 1):
                        last = mm(r[:, i * HEADS:i * HEADS + HEADS], utri[:, j, i * P:i * P + P], lg[:, j, :], start=(j == 0), stop=(j == i))
                last.then_inc(region_filled, 1)
                pe.wait_ge(relu_ready, TT * (l + 1))
                for h in range(HEADS):
                    for j in range(TT):
                        last = mm(pair(0)[:, h * T:h * T + T], nlogf[:, j, h, :], utri[:, j, :], start=(j == 0), stop=(j == TT - 1))
                last.then_inc(cb_ready, 1)
                pe.wait_ge(latent_ready, l + 1)
                b = load()
                wq = b.rearrange("p k c -> p (k c)").rearrange("p (k h c) -> p k h c", k=2, h=HEADS)
                for h in range(HEADS):
                    r = free_region(l, f"qB{h}")
                    for k in range(2):
                        last = mm(r, wq[:, k, h, :], cqn[:, k, :], start=(k == 0), stop=(k == 1))
                        if k == 0:
                            free_block(last)
                    last.then_inc(region_filled, 1)
                to_free[0] += 1
                b = load()
                wkv = b.rearrange("p k c -> p (k c)")
                for h in range(HEADS):
                    r = free_region(l, f"kB{h}")
                    mm(r[0:NOPE], wkv[:, h * NOPE:h * NOPE + NOPE], ckvn, start=True, stop=True).then_inc(region_filled, 1)
                for i in range(TT):
                    r = free_region(l, f"vB{i}")
                    mm(r, ckvn[:, i * P:i * P + P], wkv[:, GW:2 * GW], start=True, stop=True).then_inc(region_filled, 1)
                to_free[0] += 1
                pe.wait_ge(x5_ready, l + 1)
                for m in range(2):
                    r = free_region(l, f"y5_{m}")
                    for j in range(4):
                        jj = 4 * m + j
                        for c, (w, x5) in enumerate(((csre, vre), (csim, vim))):
                            last = mm(r[C5 * j:C5 * j + C5], w[:, jj, :], x5[:, jj * T:jj * T + T], start=(c == 0), stop=(c == 1))
                    last.then_inc(region_filled, 1)
                pe.wait_ge(g5_ready, 2 * (l + 1))
                for m in range(2):
                    r = free_region(l, f"glu{m}")
                    for k in range(2):
                        last = mm(r, wglu[:, k, m * P:m * P + P], g5[:, k, :], start=(k == 0), stop=(k == 1))
                    last.then_inc(region_filled, 1)
                pe.wait_ge(sq5_ready, l + 1)
                sums_of(l, "ss5", sg5, 2)

                def logits(n):
                    grp, i = n // 2, n % 2
                    u = 6 * l + n
                    if n == 0:
                        pe.wait_ge(act_taken, taken_count(l, "fk1")[1])
                        pe.wait_ge(relu_ready, TT * (l + 1))
                    if n == 1:
                        pe.wait_ge(mc_ready, l + 1)
                    if n >= 2:
                        pe.wait_ge(pt_taken, (u - 1) * 2)
                    if n == 2:
                        pe.wait_ge(act_taken, taken_count(l, "kB3")[1])
                        pe.wait_ge(dve_taken, taken_count(l, "qB3")[1])
                        pe.wait_ge(kr_ready, l + 1)
                    qo, ko = [(lambda h: half(fq[:, h // 2, :], h), lambda h: half(fk[:, h // 2, :], h)),
                              (lambda h: qB[:, h, :], lambda h: kB[:, h, :]),
                              (lambda h: half(aq[:, h // 2, :], h), lambda h: half(ak[:, h // 2, :], h))][grp]
                    head_logits((n + 1) % 2, i, qo, ko).then_inc(logits_ready, 1)

                def weighted(n):
                    grp, i = n // 2, n % 2
                    u = 6 * l + n
                    val = [fv, vB, av][grp]
                    pe.wait_ge(probs_ready, u + 1)
                    for b2 in range(2):
                        for q in (2 * b2, 2 * b2 + 1):
                            for j in range(i + 1):
                                last = nc.tensor.transpose(turned((n + 1) % 2)[:, q, j, :], soft[:, i, q, j * P:j * P + P], ident)
                        last.then_inc(pt_ready, 1)
                    for q in range(HEADS):
                        h = PERM[q]
                        if q % 2 == 0:
                            pe.wait_ge(pt_taken, u * 2 + q // 2 + 1)
                        if q == 0 and u >= 2:
                            pe.wait_ge(pv_taken, u - 1)
                        for j in range(i + 1):
                            last = mm(bank[:, 6 + i, h * HD:h * HD + HD], pT[:, q, j, :], val[:, j, h * HD:h * HD + HD],
                                      start=(j == 0), stop=(j == i))
                    last.then_inc(pv_done, 1)

                def turn(n):
                    u = 6 * l + n
                    pe.wait_ge(yn_ready, u + 1)
                    r = free_region(l, f"yt{n}")
                    for k in range(2):
                        last = nc.tensor.transpose(r[:, k * P:k * P + P], yrow[:, n % 2, k * P:k * P + P], ident)
                    last.then_inc(region_filled, 1)

                for n in range(7):
                    if n < 6:
                        logits(n)
                    if n:
                        weighted(n - 1)
                    if n >= 2:
                        turn(n - 2)
                turn(5)
                pe.wait_ge(act_taken, taken_count(l, "yt5")[1])
                for m in range(KT):
                    b = load()
                    r = free_region(l, f"out{m}")
                    for k in range(KT):
                        last = mm(r, b[:, k, :], ynT[:, k, :], start=(k == 0), stop=(k == KT - 1))
                        if k == 0:
                            free_block(last)
                    last.then_inc(region_filled, 1)
                    to_free[0] += 1
                pe.wait_ge(sq_ready, 2 * l + 2)
                sums_of(l, "ss2", sq, KT)
                pe.wait_ge(h_ready, 2 * KT * (l + 1))
                sk = [small_of(l, "sk1"), small_of(l, "sk2")]

                def keys(h):
                    pe.wait_ge(act_taken, taken_count(l, f"pq{h}_1")[1])
                    for i in range(TT):
                        r = free_region(l, f"sc{h}_{i}")
                        for w in range(2):
                            last = mm(r[:, w * P:w * P + P], qT[:, 2 * (h % 2) + w, i * P:i * P + P], sk[w], start=True, stop=True)
                            if w == 0:
                                free_block(last)
                        last.then_inc(region_filled, 1)

                for h in range(PH):
                    for w in range(2):
                        transposed(f"pq{h}_{w}")
                    keys(h)
                pe.wait_ge(act_taken, taken_count(l, f"sc{PH - 1}_1")[1])
                n0 = n_block[0]
                pairs = KEYS // 2 * l

                def expert_rows(i, first_turn):
                    for j in range(RING):
                        s = (n0 + j) % RING
                        pe.wait_ge(slot_filled[s], i * 16 + 16 * ((n0 + j) // RING + 1))
                        b = ring[:, s, :].rearrange("p (k c) -> p k c", k=KT)
                        if j % 2 == 0 and not first_turn:
                            pe.wait_ge(gelu_done, i * 4 + (pairs + j // 2 - 3))
                        for k in range(KT):
                            last = mm(bank[:, j // 2, (j % 2) * T:(j % 2) * T + T], b[:, k, :], hT[:, k, :],
                                      start=(k == 0), stop=(k == KT - 1))
                            if k == 0 and j % 2 == 0 and not (first_turn and j == 0):
                                last.then_inc(block_used, 1)
                        last.then_inc(a_ready if j % 2 else block_used, 1)

                expert_rows(0, True)
                with pe.Fori(1, KEYS // RING, 1) as i:
                    expert_rows(i, False)
                n_block[0] += KEYS
                to_free[0] = 1
                pe.wait_ge(gelu_done, KEYS // 2 * (l + 1))
                for i in range(TT):
                    pe.wait_ge(picked, TT * l + i + 1)
                    for r3 in range(3):
                        r = free_region(l, f"tr{3 * i + r3}")
                        nc.tensor.transpose(r[:, 0:P], res[:, i, r3, :], ident).then_inc(region_filled, 1)
                quads = T // 4
                q0 = quads * l
                pe.wait_ge(act_taken, taken_count(l, f"tr{3 * TT - 1}")[1])

                def gate_grids(q, j, first_turn):
                    pe.wait_ge(hot_ready, q + (q0 + 1))
                    if not first_turn:
                        pe.wait_ge(w_ready, q + (q0 - 3))
                    for t in range(4):
                        s = 4 * (j % 2) + t
                        last = mm(bank[:, j, t * P:t * P + P], hotB[:, s, :], hotA[:, s, :], start=True, stop=True)
                        if t == 0:
                            free_block(last)
                    last.then_inc(g_ready, 1)

                for j in range(4):
                    gate_grids(j, j, True)
                with pe.Fori(1, quads // 4, 1) as i:
                    for j in range(4):
                        gate_grids(i * 4 + j, j, False)
                pe.wait_ge(pv_taken, 6 * (l + 1))
                pe.wait_ge(w_ready, quads * (l + 1))
                n0 = n_block[0]
                last = None
                for b4 in range(4):
                    for hf in range(2):
                        last = mm(bank[:, 4 + b4, hf * T:hf * T + T], zeros[:, :], hT[:, 0, :], start=(hf == 0), stop=False,
                                  skip_group_check=True)
                with pe.Fori(0, KEYS // RING, 1) as i:
                    for j in range(RING):
                        s = (n0 + j) % RING
                        pe.wait_ge(slot_filled[s], i * 16 + 16 * ((n0 + j) // RING + 1))
                        for m in range(KT):
                            last = mm(bank[:, 4 + m // 2, (m % 2) * T:(m % 2) * T + T], ring[:, s, m * P:m * P + P],
                                      grid[:, bass.ds(i * (RING * T) + j * T, T)], start=False, stop=False,
                                      skip_group_check=True)
                        last.then_inc(block_used, 1)
                n_block[0] += KEYS
            pe.wait_ge(sq_ready, 2 * DEPTH + 1)
            w, c = taken_count(DEPTH - 1, REGIONS[-1][0])
            pe.wait_ge(act_taken, c)
            for k in range(KT):
                last = mm(bank[:, 0, 0:T], ones, sq[:, k, :], start=(k == 0), stop=(k == KT - 1))
            last.then_inc(region_filled, 1)


def column_block(w):
    return w.reshape(KT, P, P).transpose(1, 0, 2).reshape(P, BLOCK)


def swapped(w):
    return np.concatenate([w[:, ROPE // 2:], w[:, :ROPE // 2]], axis=1)


def layer_blocks(i, l, dst):
    n = 0
    for m in range(ADA):
        dst[n] = column_block(i["ada_w"][l][:, m * P:m * P + P])
        n += 1
    w_in = i["w_in"][l]

    def cols(name):
        return w_in[:, IN_AT[name][0]:IN_AT[name][1]]

    kr = cols("b_kr")
    wide = {"du": cols("d_u"), "iq": cols("i_q"), "aq": cols("a_q"), "ak": cols("a_k"), "av": cols("a_v"),
            "cq": cols("b_cq"), "fq": cols("c_q"), "fk": cols("c_k"), "fv": cols("c_v")}
    for name in MIX_BLOCKS:
        if name == "ik":
            b = column_block(np.concatenate([cols("i_k"), cols("i_k")], axis=1))
        elif name == "ckv":
            b = column_block(cols("b_ckv"))
        elif name == "kr":
            b = column_block(np.concatenate([kr, kr, swapped(kr), swapped(kr)], axis=1))
        elif name in ("B0", "B1"):
            m = int(name[1])
            b = np.zeros((P, 2, 4, P), np.float32)
            for part, w in enumerate((i["s5_B_re"][l], i["s5_B_im"][l])):
                for gg in range(8):
                    s = (gg % 2) * 64
                    b[gg * 16:gg * 16 + 16, part, gg // 2, s:s + 64] = w[8 * m + gg].T
            b = b.reshape(P, BLOCK)
        elif name == "UQ":
            w = i["mla_w_uq"][l].reshape(2, P, HEADS, NOPE + ROPE)
            x1, x2 = w[..., NOPE:NOPE + ROPE // 2], w[..., NOPE + ROPE // 2:]
            b = np.concatenate([w, x2, x1], axis=-1).transpose(1, 0, 2, 3).reshape(P, BLOCK)
        elif name == "UKV":
            w = i["mla_w_ukv"][l].reshape(KV_RANK, HEADS, 2, HD).transpose(0, 2, 1, 3).reshape(KV_RANK, 2 * GW)
            b = np.concatenate([w, np.zeros((P, BLOCK - 2 * GW), np.float32)], axis=1)
        else:
            k = int(name[2])
            b = column_block(wide[name[:2]][:, k * P:k * P + P])
        dst[n] = b
        n += 1
    for m in range(KT):
        dst[n] = column_block(i["w_out"][l][:, m * P:m * P + P])
        n += 1
    for m in range(PQ):
        dst[n] = column_block(i["peer_w_q"][l][:, m * P:m * P + P])
        n += 1
    dst[n:n + KEYS] = i["peer_u"][l].reshape(KEYS, P, KT, P).transpose(0, 3, 2, 1).reshape(KEYS, P, BLOCK)
    n += KEYS
    dst[n:n + KEYS] = i["peer_v"][l].reshape(KEYS, P, BLOCK)


def small_columns(i, l):
    s = np.zeros((P, N_SMALL), np.float32)

    def put(name, a):
        s[:, SMALL_AT[name][0]:SMALL_AT[name][1]] = a

    def feat(v):
        return v.reshape(-1, P).T

    put("n1g", feat(i["norm1_g"][l]))
    put("n2g", feat(i["norm2_g"][l]))
    put("adab", feat(i["ada_b"][l]))
    put("qg", feat(i["mla_q_norm_g"][l]))
    put("kvg", feat(i["mla_kv_norm_g"][l]))
    put("gng", feat(i["group_norm_g"][l]))
    put("lre", feat(i["s5_A_re"][l].reshape(-1)))
    put("lim", feat(i["s5_A_im"][l].reshape(-1)))
    put("ldt", feat(np.repeat(i["s5_log_dt"][l], 64)))
    put("D", feat(i["s5_D"][l]))
    put("bglu", feat(i["s5_b_glu"][l]))
    w = i["w_in"][l]
    w8 = np.concatenate([w[:, IN_AT["i_w"][0]:IN_AT["i_w"][1]], w[:, IN_AT["c_f"][0]:IN_AT["c_f"][1]]], axis=1)
    put("iwcf", w8.reshape(KT, P, 8).transpose(1, 0, 2).reshape(P, KT * 8))
    put("bf", np.broadcast_to(i["fox_b_f"][l][None, :], (P, HEADS)))
    put("sk1", i["peer_subkeys1"][l].T)
    put("sk2", i["peer_subkeys2"][l].T)
    return s


def s5_columns(i, l):
    s = np.zeros((P, 1024), np.float32)
    for part, w in enumerate((i["s5_C_re"][l], i["s5_C_im"][l])):
        for gg in range(16):
            j, r = gg // 2, (gg % 2) * 64
            at = part * 256 + j * C5 + (gg % 2) * 16
            s[r:r + 64, at:at + 16] = w[gg].T
    s[:, 512:] = i["s5_w_glu"][l].reshape(2, P, GW).transpose(1, 0, 2).reshape(P, 512)
    return s


def kernel(**inputs):
    import concourse.bacc as _bacc
    from concourse.bass_utils import run_bass_kernel_spmd as _run

    i = {n: np.asarray(v) for n, v in inputs.items()}
    stream = np.empty((N_BLOCKS, P, BLOCK), np.float32)
    for l in range(DEPTH):
        layer_blocks(i, l, stream[l * LAYER_BLOCKS:(l + 1) * LAYER_BLOCKS])
    s5w = np.stack([s5_columns(i, l) for l in range(DEPTH)])
    small = np.stack([small_columns(i, l) for l in range(DEPTH)], axis=1)
    vec = np.concatenate([i["c"].reshape(KT, P).T, i["final_g"].reshape(KT, P).T,
                          np.broadcast_to(i["rel_bias"].reshape(1, -1), (P, BUCKETS * HEADS))], axis=1)
    p = i["positions"].reshape(T)
    pos = np.concatenate([np.broadcast_to(p[None, :], (P, T)), p.reshape(TT, P).T], axis=1)
    x = i["x"].reshape(T, KT, P).transpose(2, 1, 0)
    arrays = {"stream": stream, "s5w": s5w, "consts": constants(), "small": small, "vec": vec, "pos": pos, "x_in": x}
    arrays = {n: np.ascontiguousarray(a) for n, a in arrays.items()}
    nc = _bacc.Bacc("TRN2", target_bir_lowering=False, num_devices=1, dynamic_dma_scratch_size=1024)
    args = [nc.dram_tensor(n, a.shape, mybir.dt.from_np(a.dtype), kind="ExternalInput").ap() for n, a in arrays.items()]
    args.append(nc.dram_tensor("y_out", (P, KT, T), F32, kind="ExternalOutput").ap())
    build(nc, *args)
    r = _run(nc, [arrays], core_ids=[0])
    y = r.results[0]["y_out"]
    return y.transpose(2, 1, 0).reshape(1, T, D)
```

```python
from contextlib import ExitStack

import numpy as np

import concourse.bass as bass
from concourse import mybir

F32 = mybir.dt.float32
F32R = mybir.dt.float32r
I32 = mybir.dt.int32
U32 = mybir.dt.uint32
ALU = mybir.AluOpType
ACT = mybir.ActivationFunctionType
AX_X = mybir.AxisListType.X

P = 128
DEPTH = 2
D = 1024
KT = D // P
T = 256
TT = T // P
GW = 256
HEADS = 4
HD = 64
KV_RANK = 128
NOPE = 64
ROPE = 32
EPS = 1e-6
TOPK = 64
BUCKETS = 32
MAX_DIST = 128
NS5 = 8
C5 = 32
PH = 8
PK = 16
KEYS = 128
BIG = 1.0e30
TAKEN = -3.0e38
BLOCK = KT * P
RING = 4
SPLIT = 4

IN_NAMES = ["a_q", "a_k", "a_v", "i_q", "i_k", "i_w", "b_cq", "b_ckv", "b_kr", "c_q", "c_k", "c_v", "c_f", "d_u"]
IN_SIZES = [GW, GW, GW, HEADS * HD, HD, HEADS, GW, KV_RANK, ROPE, GW, GW, GW, HEADS, GW]
IN_AT = dict(zip(IN_NAMES, [(int(e - s), int(e)) for e, s in zip(np.cumsum(IN_SIZES), IN_SIZES)]))

PERM = [0, 2, 1, 3]

MIX_BLOCKS = ["du0", "du1", "iq0", "iq1", "ik", "B0", "aq0", "aq1", "ak0", "ak1", "B1", "av0", "av1",
              "cq0", "cq1", "ckv", "kr", "fq0", "fq1", "fk0", "fk1", "fv0", "fv1", "UQ", "UKV"]
ADA = 6 * KT
PQ = 2 * PH
MIX = len(MIX_BLOCKS) + KT
LAYER_BLOCKS = MIX + PQ + 2 * KEYS
N_MAIN = ADA + DEPTH * LAYER_BLOCKS
N_BLOCKS = N_MAIN + (DEPTH - 1) * ADA
EARLY = PQ + KEYS + SPLIT
LATE = KEYS - SPLIT

REGIONS = [("ss1", "act")]
REGIONS += [(n, "act") for n in ["du0", "du1", "iq0", "iq1", "ik", "aq0", "aq1", "ak0", "ak1", "av0", "av1", "iwcf",
                                 "cq0", "cq1", "ckv", "krA", "krB", "fq0", "ssq", "sskv", "fq1", "fk0", "fk1", "fv0", "fv1",
                                 "fcum"]]
REGIONS += [(f"qB{h}", "dve") for h in range(HEADS)] + [(f"kB{h}", "act") for h in range(HEADS)]
REGIONS += [("vB0", "act"), ("vB1", "act")]
REGIONS += [("y5_0", "dve"), ("y5_1", "dve"), ("glu0", "act"), ("glu1", "act"), ("ss5", "act")]
REGIONS += [(f"yt{n}", "act") for n in range(6)]
REGIONS += [(f"out{m}", "dve") for m in range(KT)] + [("ss2", "act")]
for _h in range(PH + 1):
    REGIONS += [(f"pq{_h}_{w}", "act") for w in range(2) if _h < PH]
    REGIONS += [(f"sc{_h - 1}_{i}", "act") for i in range(TT) if _h]
N_REG = len(REGIONS)
REG_POS = {n: i for i, (n, _) in enumerate(REGIONS)}
PER_TAKER = {w: sum(t == w for _, t in REGIONS) for w in ("act", "dve")}


def taken_count(layer, name):
    i = REG_POS[name]
    w = REGIONS[i][1]
    return w, layer * PER_TAKER[w] + sum(t == w for _, t in REGIONS[:i + 1])


def columns(sizes):
    at, out = 0, {}
    for name, n in sizes:
        out[name] = (at, at + n)
        at += n
    return out, at


CONST_AT, N_CONST = columns([("ident", P), ("ones", P), ("iota", P),
                             ("freq", 3), ("phase", 3), ("mul", 3), ("thr", BUCKETS - 1), ("neghalf", TT)])
MIXC_AT, N_MIXC = columns([("utri", TT * T), ("causal", P + T), ("time", T)])
SMALL_AT, N_SMALL = columns([("n1g", KT), ("n2g", KT), ("adab", ADA), ("qg", 2), ("kvg", 1), ("gng", KT), ("lre", NS5),
                             ("lim", NS5), ("ldt", NS5), ("D", 2), ("bglu", 2), ("iwcf", KT * 8), ("bf", HEADS),
                             ("sk1", P), ("sk2", P)])
VEC_AT, N_VEC = columns([("c", KT), ("fg", KT), ("rel", BUCKETS * HEADS)])

INV2PI = float(np.float32(1 / (2 * np.pi)))
TWOPI = 6.283185
PI = 3.1415925
MAGIC = 12582912.0
C1 = 6.28125
C2 = float(np.float32(np.round((2 * np.pi - C1) * 2 ** 20) / 2 ** 20))
C3 = float(np.float32(2 * np.pi - C1 - C2))


def constants():
    k = np.zeros((P, N_CONST), np.float32)
    km = np.zeros((P, N_MIXC), np.float32)

    def put(name, v):
        a, at = (k, CONST_AT) if name in CONST_AT else (km, MIXC_AT)
        a[:, at[name][0]:at[name][1]] = v
    p = np.arange(P)
    t = np.arange(T)
    put("ident", np.eye(P))
    put("ones", 1.0)
    put("utri", np.concatenate([(p[:, None] + P * j <= t[None, :]) for j in range(TT)], axis=1))
    put("causal", np.concatenate([np.where(p[:, None] >= p[None, :], 0.0, -BIG),
                                  np.where(P + p[:, None] >= t[None, :], 0.0, -BIG)], axis=1))
    put("iota", p[None, :])
    put("time", t[None, :])
    half = ROPE // 2
    f = (np.float32(10000.0) ** (-(np.arange(half, dtype=np.float32)) / np.float32(half))).astype(np.float32)
    rows = f[p % half]
    scale = (NOPE + ROPE) ** -0.5
    sign = np.where(p % ROPE < half, -1.0, 1.0)
    put("freq", np.stack([np.where(p < NOPE, 0.0, rows), rows, rows], axis=1))
    put("phase", np.stack([np.where(p < NOPE + ROPE, np.pi / 2, 0.0), np.full(P, np.pi / 2), np.zeros(P)], axis=1))
    put("mul", np.stack([np.where(p < NOPE + ROPE, scale, scale * sign), np.ones(P), sign], axis=1))
    exact = BUCKETS // 2
    thr = [b if b < exact else int(np.ceil(exact * (MAX_DIST / exact) ** ((b - exact) / (BUCKETS - exact)) - 1e-9))
           for b in range(1, BUCKETS)]
    put("thr", np.array(thr)[None, :])
    put("neghalf", -0.5)
    return k, km


def build(nc, stream, s5w, consts, mixc, small, vec, pos, x_in, out):
    with ExitStack() as ctx:
        def sb(name, shape, dt=F32):
            return ctx.enter_context(nc.sbuf_tensor(name, shape, dt))

        def sem(name):
            return ctx.enter_context(nc.semaphore(name))

        base = (nc.sbuf_base + 31) // 32 * 32
        ctx.enter_context(nc.sbuf_tensor("slab", [P, 20480], F32))

        def at_byte(name, at, shape, dt=F32):
            return nc.alloc_sbuf_tensor_at(name, [P] + shape, dt, offset=base + at, align_bytes=32)

        KB = 1024
        ring = at_byte("ring", 0, [RING, BLOCK])
        split_hi = at_byte("split_hi", 16 * KB, [SPLIT, BLOCK], F32R)
        split_lo = at_byte("split_lo", 32 * KB, [SPLIT, BLOCK], F32R)
        tables = at_byte("tables", 16 * KB, [HEADS * (P + T) + 3 * T])
        KM = at_byte("KM", 26 * KB, [N_MIXC])
        s5raw = at_byte("s5raw", 32 * KB, [1024])
        hT = at_byte("hT", 48 * KB, [KT, T])
        h_hi = at_byte("h_hi", 48 * KB, [KT, T], F32R)
        w_hi = at_byte("w_hi", 48 * KB, [SPLIT, T], F32R)
        w_lo = at_byte("w_lo", 52 * KB, [SPLIT, T], F32R)
        stage = at_byte("stage", 56 * KB, [2048])
        h_lo = at_byte("h_lo", 56 * KB, [KT, T], F32R)
        hots = [at_byte("hots0", 72 * KB, [2, 8, P]), at_byte("hots1", 56 * KB, [2, 8, P])]
        ada_ring = at_byte("ada_ring", 56 * KB, [2, BLOCK])
        pick = at_byte("pick", 64 * KB, [3, T])
        res = at_byte("res", 67 * KB, [TT, 3, P])
        ada_acc = at_byte("ada_acc", 64 * KB, [BLOCK])
        zeros = at_byte("zeros", 70 * KB, [P])
        ynT = hT
        t5 = tables[:, 0:HEADS * (P + T)].rearrange("p (q s) -> p q s", q=HEADS)
        rope = tables[:, HEADS * (P + T):].rearrange("p (r t) -> p r t", r=3)
        xT = sb("xT", [P, KT, T])
        grid = sb("grid", [P, KEYS * T])
        K = sb("K", [P, N_CONST])
        S = sb("S", [P, DEPTH, N_SMALL])
        V = sb("V", [P, N_VEC])
        mod2 = sb("mod2", [P, DEPTH, ADA])
        tiny = sb("tiny", [P, 216])

        def g(at, *shape):
            n = int(np.prod(shape))
            v = grid[:, at:at + n]
            if len(shape) == 2:
                v = v.rearrange("p (a b) -> p a b", a=shape[0])
            if len(shape) == 3:
                v = v.rearrange("p (a b c) -> p a b c", a=shape[0], b=shape[1])
            return v

        du = g(0, 2, T)
        iq = g(512, 2, T)
        ik = g(1024, T)
        aq = g(1280, 2, T)
        ak = g(1792, 2, T)
        av = g(2304, TT, GW)
        cq = g(2816, 2, T)
        ckv = g(3328, T)
        krA = g(3584, T)
        krB = g(3840, T)
        fq = g(4096, 2, T)
        fk = g(4608, 2, T)
        fv = g(5120, TT, GW)
        iwcf = g(5632, TT, 8)
        sq = g(5696, KT, T)
        soft = g(5696, 2, HEADS, T)
        phase = g(8192, NS5 * T)
        tmp = g(10240, NS5 * T)
        cosT = g(12288, NS5 * T)
        sinT = g(14336, NS5 * T)
        vre = g(16384, NS5 * T)
        vim = g(18432, NS5 * T)
        zre = g(20480, NS5 * T)
        zim = g(22528, NS5 * T)
        y5 = g(8192, 2, T)
        g5 = g(8704, 2, T)
        sg5 = g(9216, 2, T)
        o5 = g(9728, 2, T)
        rot = g(10240, 1024)
        sqB = g(11264, 3, T)
        turned_sin = g(25344, NS5 * T)
        cqn = g(24576, 2, T)
        ckvn = g(25088, T)
        qB = g(25344, HEADS, T)
        kB = g(26368, HEADS, T)
        vB = g(27392, TT, GW)
        mA = g(27904, HEADS, P + T)
        mC = g(29440, HEADS, P + T)
        score = g(30976, T)
        work = g(31232, T)
        rstd = g(31488, T)
        rstdB = g(31744, 2, T)
        nlogf = g(8192, TT, HEADS, P)
        yrow = stage[:, 1024:1536].rearrange("p (a b) -> p a b", a=2)
        s5c = stage[:, 1536:2048]
        pT = stage[:, 0:1024].rearrange("p (q j t) -> p q j t", q=4, j=2)
        cre = s5raw[:, 0:256].rearrange("p (j c) -> p j c", j=NS5)
        cim = s5raw[:, 256:512].rearrange("p (j c) -> p j c", j=NS5)
        wglu = s5raw[:, 512:1024].rearrange("p (k o) -> p k o", k=2)
        csre = s5c[:, 0:256].rearrange("p (j c) -> p j c", j=NS5)
        csim = s5c[:, 256:512].rearrange("p (j c) -> p j c", j=NS5)

        scores = g(104 * T, 2 * PH, 2 * P)
        onehot = g(120 * T, 2048)
        qT = sq

        tpos = [0]

        def tn(n):
            tpos[0] += n
            return tiny[:, tpos[0] - n:tpos[0]]

        siluc = tn(KT)
        sc1 = tn(KT)
        sc2 = tn(KT)
        dt5, lr5, th5, mag5, phi5, phh5, phl5, ta5, tb5, tc5, cre5, cim5 = [tn(NS5) for _ in range(12)]
        zf = tn(TT * HEADS)
        mnf = tn(TT * HEADS)
        azf = tn(TT * HEADS)
        lf = tn(TT * HEADS)
        logf = tn(TT * HEADS)
        cumf = tn(TT * HEADS)
        nmx = tn(2 * HEADS)
        sums = tn(2 * HEADS)
        rs = tn(2 * HEADS)
        yss = tn(2)
        yrs = tn(2)
        v8 = tn(8)
        posc = tn(2)
        epst = tn(1)
        zero = tn(1)
        drel = at_byte("drel", 70 * KB + 512, [(BUCKETS - 1) * HEADS])
        drel_hi = at_byte("drel_hi", 71 * KB, [(BUCKETS - 1) * HEADS], F32R)
        drel_lo = at_byte("drel_lo", 71 * KB + 512, [(BUCKETS - 1) * HEADS])
        wk = at_byte("wk", 71 * KB, [256])
        vals = at_byte("vals", 72 * KB, [PH, 2, PK])
        idxu = at_byte("idxu", 73 * KB, [PH, 2, PK], U32)
        vc = at_byte("vc", 74 * KB, [TT, PH, PK])
        idxf = at_byte("idxf", 75 * KB, [PH, 2, PK])
        icf = at_byte("icf", 76 * KB, [2, PH, PK])
        icu = at_byte("icu", 77 * KB, [PH, PK], U32)
        icu2 = at_byte("icu2", 77 * KB + 512, [PH, PK], U32)
        gsum = tn(PH)
        posi = grid[:, 4096:4096 + T + TT].bitcast(I32)
        posf = g(0, T)
        ang = g(512, 3, T)
        kk = g(1536, 3, T)
        kw = g(2560, 3, T)
        dist = g(29440, P + T)
        FIRST = BUCKETS - 1 - 4 * (ADA // KT)
        ge = at_byte("ge", 32 * KB, [FIRST, P + T], F32R)
        diag = at_byte("diag", 48 * KB, [2, HEADS, 2, P], F32R)
        ACC0 = 8192

        def const(name):
            if name in MIXC_AT:
                return KM[:, MIXC_AT[name][0]:MIXC_AT[name][1]]
            return K[:, CONST_AT[name][0]:CONST_AT[name][1]]

        def small_of(l, name):
            return S[:, l, SMALL_AT[name][0]:SMALL_AT[name][1]]

        ident, ones, iota = const("ident"), const("ones"), const("iota")
        utri = const("utri").rearrange("p (j t) -> p j t", j=TT)
        causal = const("causal")

        bank = ctx.enter_context(nc.psum_tensor("bank", [P, 8, 512], F32))

        def region(p):
            return bank[:, p % 2, 0:T]

        def pair(w):
            return bank[:, 2 + 2 * w:4 + 2 * w, :].rearrange("p b c -> p (b c)")

        def turned(w):
            return pair(w).rearrange("p (q j t) -> p q j t", q=HEADS, j=TT)

        const_in, small_in, vec_in, pos_in, x_loaded = (sem(n) for n in ("const_in", "small_in", "vec_in", "pos_in", "x_loaded"))
        slot_filled = [sem(f"slot_filled{i}") for i in range(RING)]
        block_used = sem("block_used")
        s5w_in = sem("s5w_in")
        silu_ready = sem("silu_ready")
        region_filled, act_taken, dve_taken = sem("region_filled"), sem("act_taken"), sem("dve_taken")
        sq_ready, xr_ready, h_ready = sem("sq_ready"), sem("xr_ready"), sem("h_ready")
        rope_arg, rope_sin, rope_ready = sem("rope_arg"), sem("rope_sin"), sem("rope_ready")
        s5_exp, s5_lr, s5_mag, trig_arg, trig_ready, trig_arg2 = (sem(n) for n in ("s5_exp", "s5_lr", "s5_mag", "trig_arg", "trig_ready", "trig_arg2"))
        scanned, im_step, im_ready = sem("scanned"), sem("im_step"), sem("im_ready")
        bu_ready, bu_taken, re_ready = sem("bu_ready"), sem("bu_taken"), sem("re_ready")
        g5_ready, sq5_ready = sem("g5_ready"), sem("sq5_ready")
        sqB_ready, latent_ready = sem("sqB_ready"), sem("latent_ready")
        f_abs, f_exp, f_log, logf_ready, cb_ready, mc_ready = (sem(n) for n in ("f_abs", "f_exp", "f_log", "logf_ready", "cb_ready", "mc_ready"))
        dots_ready, relu_ready = sem("dots_ready"), sem("relu_ready")
        logits_ready, logits_taken, max_ready, probs_ready = (sem(n) for n in ("logits_ready", "logits_taken", "max_ready", "probs_ready"))
        pt_ready, pt_taken, pv_done, pv_taken = sem("pt_ready"), sem("pt_taken"), sem("pv_done"), sem("pv_taken")
        yss_ready, yrs_ready, yn_ready = sem("yss_ready"), sem("yrs_ready"), sem("yn_ready")
        kr_ready = sem("kr_ready")
        gate_max, gate_exp, picked, pick_ready = sem("gate_max"), sem("gate_exp"), sem("picked"), sem("pick_ready")
        a_ready, gelu_done = sem("a_ready"), sem("gelu_done")
        hot_ready, g_ready, w_ready = sem("hot_ready"), sem("g_ready"), sem("w_ready")
        x_done = sem("x_done")
        out_ready, out_stored = sem("out_ready"), sem("out_stored")
        dve_step, act_step, zero_ready = sem("dve_step"), sem("act_step"), sem("zero_ready")
        dist_ready, ge_ready, diag_ready, bucket_added, t5_ready = (sem(n) for n in ("dist_ready", "ge_ready", "diag_ready", "bucket_added", "t5_ready"))

        hotA = [t[:, 0, :, :] for t in hots]
        hotB = [t[:, 1, :, :] for t in hots]
        spilled, mixc_in, tables_in = (sem(n) for n in ("spilled", "mixc_in", "tables_in"))
        ada_used, ada_scaled, ada_columns = (sem(n) for n in ("ada_used", "ada_scaled", "ada_columns"))
        ada_filled = [sem(f"ada_filled{i}") for i in range(2)]
        hi_ready, lo_ready, h_split = sem("hi_ready"), sem("lo_ready"), sem("h_split")
        vhi_ready, v_ready, v_used = sem("vhi_ready"), sem("v_ready"), sem("v_used")
        hot_eq, hot_step, column_ready, turned_picks = (sem(n) for n in ("hot_eq", "hot_step", "column_ready", "turned_picks"))
        spill = nc.dram_tensor("spill", (P, HEADS * (P + T) + 3 * T), F32).ap()

        block = ctx.enter_context(nc.Block())

        def mix_at(l):
            return ADA + l * LAYER_BLOCKS

        def early_at(l):
            return mix_at(l) + MIX

        @block.sync
        def _(sp):
            sp.dma_start(V[:, :], vec).then_inc(vec_in, 16)
            for s in range(RING):
                sp.dma_start(ring[:, s, :], stream[s]).then_inc(slot_filled[s], 16)
                if s == 1:
                    sp.dma_start(K[:, :], consts).then_inc(const_in, 16)
                    sp.dma_start(posi, pos).then_inc(pos_in, 16)
                    sp.dma_start(S[:, :, :], small).then_inc(small_in, 16)
            sp.dma_start(KM[:, :], mixc).then_inc(mixc_in, 16)
            sp.dma_start(xT[:, :, :], x_in).then_inc(x_loaded, 16)

            def fetch(n, s):
                return sp.dma_start(ring[:, s, :], stream[bass.ds(n, 1)].rearrange("o p c -> (o p) c")).then_inc(slot_filled[s], 16)

            def segment(first, count, used, base):
                turns = count // RING
                with sp.Fori(0, turns, 1) as i:
                    for j in range(RING):
                        sp.wait_ge(used, i * RING + (base + j + 1))
                        fetch(i * RING + (first + j), (first + j) % RING)
                for j in range(turns * RING, count):
                    sp.wait_ge(used, base + j + 1)
                    sp.dma_start(ring[:, (first + j) % RING, :], stream[first + j]).then_inc(slot_filled[(first + j) % RING], 16)

            segment(RING, ADA, ada_used, 0)
            for l in range(DEPTH):
                segment(mix_at(l) + RING, MIX, block_used, l * MIX)
                segment(early_at(l) + RING, EARLY, lo_ready, l * EARLY)
                late = early_at(l) + EARLY
                if l + 1 == DEPTH:
                    segment(late + RING, LATE - RING, v_ready, l * KEYS + SPLIT)
                    break
                sp.wait_ge(w_ready, T // 4 * (l + 1))
                ada_turns = (0, 1, 4, 6, 8, 10, 12, 14)
                with sp.Fori(0, ADA // KT, 1) as i:
                    for j in range(20):
                        sp.wait_ge(v_ready, i * 20 + (l * KEYS + SPLIT + j + 1))
                        fetch(i * 20 + (late + RING + j), (late + RING + j) % RING)
                        if j in ada_turns:
                            k = ada_turns.index(j)
                            sp.wait_ge(ada_used, i * 8 + (ADA + k - 1))
                            sp.dma_start(ada_ring[:, k % 2, :], stream[bass.ds(i * 8 + (N_MAIN + l * ADA + k), 1)]
                                         .rearrange("o p c -> (o p) c")).then_inc(ada_filled[k % 2], 16)
                segment(late + RING + 120, LATE - 120, v_ready, l * KEYS + SPLIT + 120)
            sp.wait_ge(out_ready, 1)
            sp.dma_start(out, hT[:, :, :]).then_inc(out_stored, 16)
            sp.wait_ge(out_stored, 16)

        @block.gpsimd
        def _(pool):
            gp = nc.gpsimd
            for l in range(DEPTH):
                pool.wait_ge(scanned, l + 1)
                gp.tensor_tensor(vim, cosT, zim, ALU.mult)
                gp.tensor_tensor(turned_sin, sinT, zre, ALU.mult).then_inc(im_step, 1)
                pool.wait_ge(im_step, l + 1)
                gp.tensor_tensor(vim, vim, turned_sin, ALU.add).then_inc(im_ready, 1)
                for n in range(6):
                    pool.wait_ge(yss_ready, 6 * l + n + 1)
                    gp.tensor_tensor(yrs[:, n % 2:n % 2 + 1], yss[:, n % 2:n % 2 + 1], const("neghalf")[:, 0:1],
                                     ALU.pow).then_inc(yrs_ready, 1)
                e0 = early_at(l)

                def low(i, j):
                    pool.wait_ge(hi_ready, i * SPLIT + (l * EARLY + j + 1))
                    gp.tensor_tensor(split_lo[:, j, :], ring[:, (e0 + j) % RING, :], split_hi[:, j, :].bitcast(F32), ALU.subtract)\
                        .then_inc(lo_ready, 1)

                with pool.Fori(0, EARLY // SPLIT, 1) as i:
                    for j in range(SPLIT):
                        low(i, j)
                q0 = T // 8 * l
                with pool.Fori(0, T // 16, 1) as i:
                    for j in range(2):
                        pool.wait_ge(hot_eq, i * 2 + (q0 + j + 1))
                        gp.tensor_tensor(hotA[j], hotA[j], pick[:, 2, bass.ds(i * 16 + 8 * j, 8)].unsqueeze(2).broadcast_to([P, 8, P]),
                                         ALU.mult).then_inc(hot_ready, 1)
                if l + 1 < DEPTH:
                    with pool.Fori(0, ADA // KT, 1) as i:
                        for k in range(KT):
                            pool.wait_ge(ada_filled[k % 2], i * (16 * KT // 2) + 16 * (k // 2 + 1))
                            silu = siluc[:, k:k + 1].broadcast_to([P, BLOCK])
                            if k == 0:
                                pool.wait_ge(ada_columns, i + ADA // KT)
                                gp.tensor_tensor(ada_acc[:, :], ada_ring[:, 0, :], silu, ALU.mult).then_inc(ada_used, 1)
                            else:
                                b = ada_ring[:, k % 2, :]
                                gp.tensor_tensor(b, b, silu, ALU.mult).then_inc(ada_scaled, 1)
                                pool.wait_ge(ada_scaled, i * (KT - 1) + k)
                                gp.tensor_tensor(ada_acc[:, :], ada_acc[:, :], b, ALU.add).then_inc(ada_used, 1)
                            pool.wait_ge(ada_used, i * KT + (ADA + k + 1))

        def out_rows(act, l, n, take):
            grp, i = n // 2, n % 2
            kt0 = [4, 2, 0][grp]
            if n == 0:
                act.wait_ge(region_filled, l * N_REG + REG_POS["fv1"] + 1)
            t = take(l, f"yt{n}")
            for k in range(2):
                last = nc.scalar.activation(ynT[:, kt0 + k, i * P:i * P + P], t[:, k * P:k * P + P], ACT.Copy,
                                            scale=small_of(l, "gng")[:, kt0 + k:kt0 + k + 1])
            last.then_inc(act_taken, 1)

        @block.scalar
        def _(act):
            steps = [0]

            def link(ins):
                steps[0] += 1
                ins.then_inc(act_step, 1)
                act.wait_ge(act_step, steps[0])

            def take(l, name):
                p = l * N_REG + REG_POS[name]
                act.wait_ge(region_filled, p + 1)
                return region(p)

            def copy(l, name, dst, scale=1.0):
                return nc.scalar.activation(dst, take(l, name)[:, 0:dst.free_size()], ACT.Copy, scale=scale)\
                    .then_inc(act_taken, 1)

            def root(l, name, n, dst):
                nc.scalar.activation(dst, take(l, name), ACT.Sqrt, bias=epst[:, 0:1], scale=1.0 / n).then_inc(act_taken, 1)

            def squares(ready, l):
                for m in range(KT):
                    if ready is x_done:
                        act.wait_ge(x_done, l * KT + m + 1)
                    nc.scalar.activation(sq[:, m, :], xT[:, m, :], ACT.Square).then_inc(sq_ready, 1)

            act.wait_ge(vec_in, 16)
            act.wait_ge(zero_ready, 1)
            nc.scalar.activation(siluc[:, :], V[:, VEC_AT["c"][0]:VEC_AT["c"][1]], ACT.Sigmoid).then_inc(silu_ready, 1)
            act.wait_ge(dist_ready, 1)
            act.wait_ge(const_in, 16)

            def diagonals(b, j):
                for q in range(HEADS):
                    for part, d in enumerate((drel_hi[:, :].bitcast(F32), drel_lo)):
                        last = nc.scalar.activation(diag[:, j, q, part, :], ident, ACT.Copy, scale=d[:, bass.ds(b * HEADS + PERM[q], 1)])
                last.then_inc(diag_ready, 1)

            for b in range(3):
                if b == 2:
                    act.wait_ge(bucket_added, 1)
                diagonals(b, b % 2)
            with act.Fori(0, (BUCKETS - 4) // 2, 1) as i:
                for j in range(2):
                    act.wait_ge(bucket_added, i * 2 + (2 + j))
                    diagonals(i * 2 + (3 + j), (3 + j) % 2)
            act.wait_ge(rope_arg, 1)
            nc.scalar.activation(rope[:, :, :], kw, ACT.Sin).then_inc(rope_sin, 1)
            act.wait_ge(bucket_added, BUCKETS - 1)
            for q in range(HEADS):
                at = VEC_AT["rel"][0] + PERM[q]
                nc.scalar.activation(t5[:, q, :], bank[:, 2 + q, 0:P + T], ACT.Identity, bias=V[:, at:at + 1]).then_inc(t5_ready, 1)
            for l in range(DEPTH):
                act.wait_ge(small_in, 16)
                if l:
                    act.wait_ge(v_used, l * KEYS)
                act.dma_start(s5raw[:, :], s5w[l]).then_inc(s5w_in, 16)
                if l:
                    act.dma_start(KM[:, :], mixc).then_inc(mixc_in, 16)
                    act.dma_start(tables[:, :], spill).then_inc(tables_in, 16)
                if l == 0:
                    act.wait_ge(x_loaded, 16)
                squares(x_done if l else x_loaded, l - 1)
                root(l, "ss1", D, rstd)
                for k in range(KT):
                    act.wait_ge(xr_ready, 2 * KT * l + k + 1)
                    nc.scalar.activation(hT[:, k, :], sq[:, k, :], ACT.Identity, bias=mod2[:, l, k:k + 1],
                                         scale=sc1[:, k:k + 1]).then_inc(h_ready, 1)
                nc.scalar.activation(dt5, small_of(l, "ldt"), ACT.Exp).then_inc(s5_exp, 1)
                copy(l, "du0", du[:, 0, :])
                act.wait_ge(s5_lr, l + 1)
                nc.scalar.activation(mag5, lr5, ACT.Exp).then_inc(s5_mag, 1)
                copy(l, "du1", du[:, 1, :])
                for i in range(2):
                    copy(l, f"iq{i}", iq[:, i, :])
                copy(l, "ik", ik)
                act.wait_ge(trig_arg, l + 1)
                nc.scalar.activation(sinT, phase, ACT.Sin, scale=TWOPI).then_inc(trig_ready, 1)
                act.wait_ge(trig_arg2, l + 1)
                nc.scalar.activation(cosT, tmp, ACT.Sin, scale=-TWOPI).then_inc(trig_ready, 1)
                for i in range(2):
                    copy(l, f"aq{i}", aq[:, i, :], HD ** -0.5)
                for i in range(2):
                    copy(l, f"ak{i}", ak[:, i, :])
                for i in range(2):
                    nc.scalar.activation(av[:, :, i * P:i * P + P], take(l, f"av{i}").rearrange("p (a b) -> p a b", a=TT),
                                         ACT.Copy).then_inc(act_taken, 1)
                copy(l, "iwcf", grid[:, 5632:5648])
                for i in range(TT):
                    w = (i + 1) * P
                    act.wait_ge(dots_ready, TT * l + i + 1)
                    nc.scalar.activation(soft[:, i, :, 0:w], pair(i).rearrange("p (q s) -> p q s", q=HEADS)[:, :, 0:w],
                                         ACT.Relu).then_inc(relu_ready, 1)
                for i in range(2):
                    copy(l, f"cq{i}", cq[:, i, :])
                copy(l, "ckv", ckv)
                act.wait_ge(act_taken, taken_count(l, "ckv")[1])
                nc.scalar.activation(sqB[:, 0:2, :], cq, ACT.Square)
                nc.scalar.activation(sqB[:, 2, :], ckv, ACT.Square).then_inc(sqB_ready, 1)
                for n, dst in (("krA", krA), ("krB", krB)):
                    nc.scalar.activation(dst[64:P], take(l, n)[64:P], ACT.Copy).then_inc(act_taken, 1)
                copy(l, "fq0", fq[:, 0, :], HD ** -0.5)
                root(l, "ssq", GW, rstdB[:, 0, :])
                root(l, "sskv", KV_RANK, rstdB[:, 1, :])
                copy(l, "fq1", fq[:, 1, :], HD ** -0.5)
                copy(l, "fk0", fk[:, 0, :])
                act.wait_ge(f_abs, l + 1)
                nc.scalar.activation(lf, azf, ACT.Exp, scale=-1.0).then_inc(f_exp, 1)
                act.wait_ge(f_exp, l + 1)
                nc.scalar.activation(lf, lf, ACT.Ln, bias=1.0).then_inc(f_log, 1)
                copy(l, "fk1", fk[:, 1, :])
                for i in range(2):
                    nc.scalar.activation(fv[:, :, i * P:i * P + P], take(l, f"fv{i}").rearrange("p (a b) -> p a b", a=TT),
                                         ACT.Copy).then_inc(act_taken, 1)
                copy(l, "fcum", cumf)
                act.wait_ge(im_ready, l + 1)
                for h in range(HEADS):
                    nc.scalar.activation(kB[0:NOPE, h, :], take(l, f"kB{h}")[0:NOPE], ACT.Copy).then_inc(act_taken, 1)
                for i in range(TT):
                    copy(l, f"vB{i}", vB[:, i, :])
                for i in range(2):
                    act.wait_ge(dve_taken, taken_count(l, f"y5_{i}")[1])
                    nc.scalar.activation(g5[:, i, :], y5[:, i, :], ACT.Gelu_apprx_tanh).then_inc(g5_ready, 1)
                for i in range(2):
                    nc.scalar.activation(sg5[:, i, :], take(l, f"glu{i}"), ACT.Sigmoid, bias=small_of(l, "bglu")[:, i:i + 1])\
                        .then_inc(act_taken, 1)
                root(l, "ss5", GW, rstd)
                for n in range(6):
                    w = (n % 2 + 1) * P
                    act.wait_ge(max_ready, 6 * l + n + 1)
                    for q in range(HEADS):
                        h = PERM[q]
                        last = nc.scalar.activation(soft[:, n % 2, q, 0:w], soft[:, n % 2, q, 0:w], ACT.Exp,
                                                    bias=nmx[:, 4 * (n % 2) + q:4 * (n % 2) + q + 1],
                                                    accum_out=sums[:, 4 * (n % 2) + h:4 * (n % 2) + h + 1])
                    last.then_inc(probs_ready, 1)
                    for b in range(2):
                        act.wait_ge(pt_ready, (6 * l + n) * 2 + b + 1)
                        j = n % 2 + 1
                        nc.scalar.activation(pT[:, 2 * b:2 * b + 2, 0:j, :], turned((n + 1) % 2)[:, 2 * b:2 * b + 2, 0:j, :],
                                             ACT.Copy).then_inc(pt_taken, 1)
                    if n:
                        out_rows(act, l, n - 1, take)
                out_rows(act, l, 5, take)
                if l == 0:
                    act.wait_ge(t5_ready, HEADS)
                    act.wait_ge(rope_ready, 1)
                    act.dma_start(spill, tables[:, :]).then_inc(spilled, 16)
                for m in range(KT):
                    act.wait_ge(dve_taken, taken_count(l, f"out{m}")[1])
                    nc.scalar.activation(sq[:, m, :], xT[:, m, :], ACT.Square).then_inc(sq_ready, 1)
                e0 = early_at(l)
                if l == 0:
                    act.wait_ge(spilled, 16)

                def high(n, i=0, turn=0):
                    act.wait_ge(slot_filled[(e0 + n) % RING], i * (16 * turn // RING) + 16 * ((e0 + n) // RING + 1))
                    nc.scalar.activation(split_hi[:, n % SPLIT, :], ring[:, (e0 + n) % RING, :], ACT.Copy).then_inc(hi_ready, 1)

                for n in range(SPLIT - 1):
                    high(n)
                root(l, "ss2", D, rstd)
                for k in range(KT):
                    act.wait_ge(xr_ready, 2 * KT * l + KT + k + 1)
                    nc.scalar.activation(sq[:, k, :], sq[:, k, :], ACT.Identity, bias=mod2[:, l, 3 * KT + k:3 * KT + k + 1],
                                         scale=sc2[:, k:k + 1]).then_inc(h_ready, 1)
                high(SPLIT - 1)
                for h in range(PH + 1):
                    for w in range(2):
                        if h < PH:
                            copy(l, f"pq{h}_{w}", qT[:, 2 * (h % 2) + w, :])
                            high(2 * h + w + SPLIT)
                    for i in range(TT):
                        if h:
                            copy(l, f"sc{h - 1}_{i}", scores[:, i * PH + h - 1, :])
                first = KEYS // 2 * l

                def gelus(i):
                    for j in range(4):
                        act.wait_ge(a_ready, i * 4 + (first + j + 1))
                        for w in range(2):
                            high(PQ + 2 * j + w + SPLIT, i, 8)
                        nc.scalar.activation(grid[:, bass.ds(i * (8 * T) + j * 2 * T, 2 * T)], bank[:, j, :],
                                             ACT.Gelu_apprx_tanh).then_inc(gelu_done, 1)

                with act.Fori(0, 9, 1) as i:
                    gelus(i)
                for i in range(TT):
                    act.wait_ge(gate_max, TT * l + i + 1)
                    nc.scalar.activation(vc[:, i, :, :], vc[:, i, :, :], ACT.Exp).then_inc(gate_exp, 1)
                with act.Fori(9, 12, 1) as i:
                    gelus(i)
                act.wait_ge(picked, TT * (l + 1))
                with act.Fori(12, 14, 1) as i:
                    gelus(i)
                act.wait_ge(turned_picks, l + 1)
                for i in range(TT):
                    nc.scalar.activation(pick[:, :, i * P:i * P + P], bank[:, 6 + i, 0:3 * P].rearrange("p (r t) -> p r t", r=3),
                                         ACT.Copy).then_inc(pick_ready, 1)
                with act.Fori(14, 16, 1) as i:
                    gelus(i)

                def column_hots(n, j):
                    for t in range(2, 8):
                        last = nc.scalar.activation(hotB[j][:, t, :], iota, ACT.Abs, scale=-1.0, bias=pick[:, 1, bass.ds(n * 8 + t, 1)])
                    last.then_inc(hot_step, 1)
                    act.wait_ge(hot_step, n + (T // 8 * l + 1))
                    nc.scalar.activation(hotB[j][:, 2:8, :], hotB[j][:, 2:8, :], ACT.Relu, scale=-1.0, bias=1.0).then_inc(column_ready, 1)

                act.wait_ge(pick_ready, TT * (l + 1))
                for n in range(2):
                    column_hots(n, n)
                with act.Fori(0, T // 16 - 1, 1) as i:
                    for j in range(2):
                        act.wait_ge(g_ready, i * 4 + (T // 4 * l + 2 * j + 2))
                        column_hots(i * 2 + (2 + j), j)
                act.wait_ge(w_ready, T // 4 * (l + 1))
                late = e0 + EARLY
                for j in range(SPLIT):
                    nc.scalar.activation(w_hi[:, j, :], grid[:, j * T:j * T + T], ACT.Copy).then_inc(vhi_ready, 1)
                with act.Fori(0, LATE // SPLIT, 1) as i:
                    for j in range(SPLIT):
                        s = (late + j) % RING
                        act.wait_ge(slot_filled[s], i * 16 + 16 * ((late + j) // RING + 1))
                        act.wait_ge(v_used, i * SPLIT + (l * KEYS + j + 1))
                        nc.scalar.activation(split_hi[:, j, :], ring[:, s, :], ACT.Copy)
                        nc.scalar.activation(w_hi[:, j, :], grid[:, bass.ds(i * (SPLIT * T) + (SPLIT + j) * T, T)], ACT.Copy)\
                            .then_inc(vhi_ready, 1)
            squares(x_done, DEPTH - 1)
            act.wait_ge(region_filled, DEPTH * N_REG + 1)
            nc.scalar.activation(rstd, bank[:, 0, 0:T], ACT.Sqrt, bias=epst[:, 0:1], scale=1.0 / D).then_inc(act_taken, 1)

        @block.vector
        def _(dve):
            v = nc.vector
            steps = [0]

            def link(ins):
                steps[0] += 1
                ins.then_inc(dve_step, 1)
                dve.wait_ge(dve_step, steps[0])

            def take(l, name):
                p = l * N_REG + REG_POS[name]
                dve.wait_ge(region_filled, p + 1)
                return region(p)

            v.memset(epst, EPS)
            v.memset(zeros[:, :], 0.0).then_inc(zero_ready, 1)
            dve.wait_ge(silu_ready, 1)
            v.tensor_tensor(siluc, siluc, V[:, VEC_AT["c"][0]:VEC_AT["c"][1]], ALU.mult).then_inc(silu_ready, 1)
            dve.wait_ge(pos_in, 16)
            dve.wait_ge(const_in, 16)
            v.tensor_copy(posf, posi[:, 0:T])
            link(v.tensor_copy(posc, posi[:, T:T + TT]))
            r0 = VEC_AT["rel"][0]
            dve.wait_ge(vec_in, 16)
            link(v.tensor_tensor(drel[:, :], V[:, r0 + HEADS:r0 + BUCKETS * HEADS], V[:, r0:r0 + (BUCKETS - 1) * HEADS], ALU.subtract))
            v.tensor_scalar(dist[:, 0:P], posf[:, 0:P], posc[:, 0:1], -1.0, ALU.subtract, ALU.mult)
            v.tensor_scalar(dist[:, P:P + T], posf, posc[:, 1:2], -1.0, ALU.subtract, ALU.mult)
            link(v.tensor_copy(drel_hi[:, :], drel[:, :]))
            v.tensor_tensor(drel_lo[:, :], drel[:, :], drel_hi[:, :].bitcast(F32), ALU.subtract).then_inc(dist_ready, 1)
            dve.wait_ge(dist_ready, 1)
            thr = CONST_AT["thr"][0]

            def reached(b, slot):
                v.tensor_scalar(ge[:, slot, :], dist, K[:, bass.ds(b + thr, 1)], None, ALU.is_ge).then_inc(ge_ready, 1)

            for b in range(FIRST):
                reached(b, b)
            for i in range(3):
                last = v.tensor_scalar(ang[:, i, :], posf, const("freq")[:, i:i + 1], None, ALU.mult)
            link(last)
            link(v.tensor_scalar(kk, ang, INV2PI, MAGIC, ALU.mult, ALU.add))
            link(v.tensor_scalar(kk, kk, -MAGIC, None, ALU.add))
            link(v.scalar_tensor_tensor(ang, kk, -C1, ang, ALU.mult, ALU.add))
            link(v.scalar_tensor_tensor(ang, kk, -C2, ang, ALU.mult, ALU.add))
            link(v.scalar_tensor_tensor(ang, kk, -C3, ang, ALU.mult, ALU.add))
            for i in range(3):
                last = v.tensor_scalar(kk[:, i, :], ang[:, i, :], const("phase")[:, i:i + 1], None, ALU.add)
            link(last)
            link(v.tensor_scalar(kw, kk, PI, -2 * PI, ALU.is_gt, ALU.mult))
            link(v.tensor_tensor(kw, kw, kk, ALU.add))
            v.tensor_scalar(kw, kw, PI, -PI, ALU.min, ALU.max).then_inc(rope_arg, 1)
            def add_biases(l, b):
                dve.wait_ge(ada_columns, ADA // KT * (l + 1))
                link(v.tensor_tensor(mod2[:, l, :], bank[:, b, 0:ADA], small_of(l, "adab"), ALU.add))

            dve.wait_ge(silu_ready, 2)
            dve.wait_ge(small_in, 16)
            with dve.Fori(0, ADA // KT, 1) as i:
                for k in range(KT):
                    dve.wait_ge(slot_filled[k % RING], i * (16 * KT // RING) + 16 * (k // RING + 1))
                    acc = grid[:, bass.ds(i * BLOCK + ACC0, BLOCK)]
                    if k == 0:
                        ins = v.tensor_scalar(acc, ring[:, 0, :], siluc[:, 0:1], None, ALU.mult)
                    else:
                        ins = v.scalar_tensor_tensor(acc, ring[:, k % RING, :], siluc[:, k:k + 1], acc, ALU.mult, ALU.add)
                    ins.then_inc(ada_used, 1)
                    if k < 4:
                        dve.wait_ge(bucket_added, i * 4 + (FIRST - 3 + k))
                        reached(i * 4 + (FIRST + k), k)
                    dve.wait_ge(ada_used, i * KT + (k + 1))
            add_biases(0, 7)
            dve.wait_ge(rope_sin, 1)
            for i in range(3):
                last = v.tensor_scalar(rope[:, i, :], rope[:, i, :], const("mul")[:, i:i + 1], None, ALU.mult)
            last.then_inc(rope_ready, 1)
            dve.wait_ge(rope_ready, 1)
            dve.wait_ge(mixc_in, 16)
            for l in range(DEPTH):
                sm = lambda n: small_of(l, n)
                dve.wait_ge(small_in, 16)
                v.scalar_tensor_tensor(sc1, mod2[:, l, KT:2 * KT], 1.0, sm("n1g"), ALU.add, ALU.mult)
                link(v.scalar_tensor_tensor(sc2, mod2[:, l, 4 * KT:5 * KT], 1.0, sm("n2g"), ALU.add, ALU.mult))

                def normed(l, which):
                    dve.wait_ge(act_taken, taken_count(l, which)[1])
                    link(v.reciprocal(rstd, rstd))
                    for k in range(KT):
                        v.tensor_tensor(sq[:, k, :], xT[:, k, :], rstd, ALU.mult).then_inc(xr_ready, 1)

                normed(l, "ss1")
                if l:
                    dve.wait_ge(mixc_in, 16 * (l + 1))
                dve.wait_ge(s5_exp, l + 1)
                v.tensor_tensor(lr5, sm("lre"), dt5, ALU.mult).then_inc(s5_lr, 1)
                link(v.tensor_tensor(th5, sm("lim"), dt5, ALU.mult))
                link(v.tensor_scalar(phi5, th5, INV2PI, None, ALU.mult))
                link(v.tensor_scalar(ta5, phi5, 4097.0, None, ALU.mult))
                link(v.tensor_tensor(tb5, ta5, phi5, ALU.subtract))
                link(v.tensor_tensor(phh5, ta5, tb5, ALU.subtract))
                link(v.tensor_tensor(phl5, phi5, phh5, ALU.subtract))
                ph3 = phase.rearrange("p (j t) -> p j t", j=NS5)
                tm3 = tmp.rearrange("p (j t) -> p j t", j=NS5)
                time = const("time").unsqueeze(1).broadcast_to([P, NS5, T])
                link(v.tensor_tensor(ph3, time, phh5.unsqueeze(2).broadcast_to([P, NS5, T]), ALU.mult))
                link(v.tensor_scalar(tmp, phase, MAGIC, -MAGIC, ALU.add, ALU.add))
                link(v.tensor_tensor(phase, phase, tmp, ALU.subtract))
                link(v.tensor_tensor(tm3, time, phl5.unsqueeze(2).broadcast_to([P, NS5, T]), ALU.mult))
                link(v.tensor_tensor(phase, phase, tmp, ALU.add))
                link(v.tensor_scalar(tmp, phase, MAGIC, -MAGIC, ALU.add, ALU.add))
                v.tensor_tensor(phase, phase, tmp, ALU.subtract).then_inc(trig_arg, 1)
                dve.wait_ge(trig_arg, l + 1)
                link(v.tensor_scalar(tmp, phase, 0.25, None, ALU.add))
                v.scalar_tensor_tensor(tmp, tmp, 0.5, tmp, ALU.is_gt, ALU.subtract).then_inc(trig_arg2, 1)

                dve.wait_ge(trig_ready, 2 * (l + 1))
                dve.wait_ge(s5_mag, l + 1)
                c3 = cosT.rearrange("p (j t) -> p j t", j=NS5)
                s3 = sinT.rearrange("p (j t) -> p j t", j=NS5)
                v.tensor_tensor(ta5, mag5, c3[:, :, 1], ALU.mult)
                link(v.tensor_tensor(tb5, mag5, s3[:, :, 1], ALU.mult))
                link(v.tensor_scalar(ta5, ta5, -1.0, None, ALU.add))
                v.tensor_tensor(cre5, ta5, sm("lre"), ALU.mult)
                v.tensor_tensor(tc5, tb5, sm("lim"), ALU.mult)
                v.tensor_tensor(cim5, tb5, sm("lre"), ALU.mult)
                link(v.tensor_tensor(phi5, ta5, sm("lim"), ALU.mult))
                v.tensor_tensor(cre5, cre5, tc5, ALU.add)
                link(v.tensor_tensor(cim5, cim5, phi5, ALU.subtract))
                v.tensor_tensor(ta5, sm("lre"), sm("lre"), ALU.mult)
                link(v.tensor_tensor(tb5, sm("lim"), sm("lim"), ALU.mult))
                link(v.tensor_tensor(ta5, ta5, tb5, ALU.add))
                link(v.reciprocal(ta5, ta5))
                v.tensor_tensor(cre5, cre5, ta5, ALU.mult)
                link(v.tensor_tensor(cim5, cim5, ta5, ALU.mult))
                dve.wait_ge(s5w_in, 16 * (l + 1))
                crb = cre5.unsqueeze(2).broadcast_to([P, NS5, C5])
                cib = cim5.unsqueeze(2).broadcast_to([P, NS5, C5])
                s5t = wk[:, :].rearrange("p (j c) -> p j c", j=NS5)
                v.tensor_tensor(csre, cre, crb, ALU.mult)
                link(v.tensor_tensor(s5t, cim, cib, ALU.mult))
                link(v.tensor_tensor(csre, csre, s5t, ALU.subtract))
                v.tensor_tensor(csim, cre, cib, ALU.mult)
                link(v.tensor_tensor(s5t, cim, crb, ALU.mult))
                link(v.scalar_tensor_tensor(csim, csim, -1.0, s5t, ALU.mult, ALU.subtract))
                for m in range(2):
                    dve.wait_ge(bu_ready, 2 * l + m + 1)
                    s = slice(1024 * m, 1024 * m + 1024)
                    br, bi = pair(0), pair(1)
                    v.tensor_tensor(vre[:, s], cosT[:, s], br, ALU.mult)
                    link(v.tensor_tensor(rot, sinT[:, s], bi, ALU.mult))
                    v.tensor_tensor(vre[:, s], vre[:, s], rot, ALU.add)
                    link(v.tensor_tensor(vim[:, s], cosT[:, s], bi, ALU.mult))
                    v.tensor_tensor(rot, sinT[:, s], br, ALU.mult).then_inc(bu_taken, 1)
                    dve.wait_ge(bu_taken, 2 * l + m + 1)
                    link(v.tensor_tensor(vim[:, s], vim[:, s], rot, ALU.subtract))
                for j in range(NS5):
                    s = slice(T * j, T * j + T)
                    m = mag5[:, j:j + 1].broadcast_to([P, T])
                    v.tensor_tensor_scan(zre[:, s], m, vre[:, s], 0.0, ALU.mult, ALU.add)
                    last = v.tensor_tensor_scan(zim[:, s], m, vim[:, s], 0.0, ALU.mult, ALU.add)
                last.then_inc(scanned, 1)
                dve.wait_ge(scanned, l + 1)
                v.tensor_tensor(vre, cosT, zre, ALU.mult)
                link(v.tensor_tensor(phase, sinT, zim, ALU.mult))
                v.tensor_tensor(vre, vre, phase, ALU.subtract).then_inc(re_ready, 1)
                dve.wait_ge(act_taken, taken_count(l, "iwcf")[1])
                z3 = zf.rearrange("p (i h) -> p i h", i=TT)
                link(v.tensor_tensor(z3, iwcf[:, :, HEADS:8], sm("bf").unsqueeze(1).broadcast_to([P, TT, HEADS]), ALU.add))
                link(v.tensor_scalar(mnf, zf, 0.0, None, ALU.min))
                link(v.tensor_scalar(azf, zf, -1.0, None, ALU.mult))
                v.tensor_tensor(azf, zf, azf, ALU.max).then_inc(f_abs, 1)
                if l:
                    dve.wait_ge(tables_in, 16 * l)
                else:
                    dve.wait_ge(t5_ready, HEADS)
                for i in range(TT):
                    w = (i + 1) * P
                    at = 0 if i == 0 else P
                    dve.wait_ge(relu_ready, TT * l + i + 1)
                    link(v.tensor_scalar(score[:, 0:w], soft[:, i, 0, 0:w], iwcf[:, i, 0:1], None, ALU.mult))
                    for q in range(1, HEADS):
                        h = PERM[q]
                        link(v.scalar_tensor_tensor(score[:, 0:w], soft[:, i, q, 0:w], iwcf[:, i, h:h + 1], score[:, 0:w],
                                                    ALU.mult, ALU.add))
                    link(v.tensor_tensor(work[:, 0:w], score[:, 0:w], causal[:, at:at + w], ALU.add))
                    for _ in range(TOPK // 8):
                        link(v.max(v8, work[:, 0:w]))
                        link(v.match_replace(work[:, 0:w], v8, work[:, 0:w], TAKEN))
                    link(v.tensor_scalar(work[:, 0:w], work[:, 0:w], TAKEN / 2, -BIG, ALU.is_ge, ALU.mult))
                    link(v.tensor_tensor(work[:, 0:w], work[:, 0:w], causal[:, at:at + w], ALU.add))
                    link(v.tensor_tensor(mA[:, :, at:at + w], t5[:, :, at:at + w],
                                         work[:, 0:w].unsqueeze(1).broadcast_to([P, HEADS, w]), ALU.add))
                dve.wait_ge(act_taken, taken_count(l, "sskv")[1])
                link(v.reciprocal(rstdB, rstdB))
                for i in range(2):
                    v.scalar_tensor_tensor(cqn[:, i, :], cq[:, i, :], sm("qg")[:, i:i + 1], rstdB[:, 0, :], ALU.mult, ALU.mult)
                v.scalar_tensor_tensor(ckvn, ckv, sm("kvg")[:, 0:1], rstdB[:, 1, :], ALU.mult, ALU.mult)\
                    .then_inc(latent_ready, 1)
                dve.wait_ge(im_ready, l + 1)
                hi = slice(64, P)
                v.tensor_tensor(krA[hi], krA[hi], rope[hi, 1, :], ALU.mult)
                link(v.tensor_tensor(krB[hi], krB[hi], rope[hi, 2, :], ALU.mult))
                link(v.tensor_tensor(krA[hi], krA[hi], krB[hi], ALU.add))
                v.tensor_copy(kB[hi, :, :], krA[hi].unsqueeze(1).broadcast_to([64, HEADS, T])).then_inc(kr_ready, 1)
                dve.wait_ge(f_log, l + 1)
                v.tensor_tensor(logf, mnf, lf, ALU.subtract)
                link(v.tensor_tensor(azf, lf, mnf, ALU.subtract))
                for i in range(TT):
                    last = v.tensor_copy(nlogf[:, i, :, :], azf[:, i * HEADS:i * HEADS + HEADS].unsqueeze(2)
                                         .broadcast_to([P, HEADS, P]))
                last.then_inc(logf_ready, 1)
                for h in range(HEADS):
                    v.tensor_tensor(qB[:, h, :], take(l, f"qB{h}"), rope[:, 0, :], ALU.mult).then_inc(dve_taken, 1)
                dve.wait_ge(cb_ready, l + 1)
                dve.wait_ge(act_taken, taken_count(l, "fcum")[1])
                for i in range(TT):
                    w = (i + 1) * P
                    at = 0 if i == 0 else P
                    for q in range(HEADS):
                        h = PERM[q]
                        last = v.scalar_tensor_tensor(mC[:, q, at:at + w], pair(0)[:, h * T:h * T + w],
                                                      cumf[:, i * HEADS + h:i * HEADS + h + 1], causal[:, at:at + w],
                                                      ALU.add, ALU.add)
                last.then_inc(mc_ready, 1)
                for i in range(2):
                    v.scalar_tensor_tensor(y5[:, i, :], du[:, i, :], sm("D")[:, i:i + 1], take(l, f"y5_{i}"), ALU.mult, ALU.add)\
                        .then_inc(dve_taken, 1)
                dve.wait_ge(act_taken, taken_count(l, "glu1")[1])
                link(v.tensor_tensor(o5, g5, sg5, ALU.mult))
                v.tensor_tensor(sg5, o5, o5, ALU.mult).then_inc(sq5_ready, 1)
                dve.wait_ge(act_taken, taken_count(l, "ss5")[1])
                link(v.reciprocal(rstd, rstd))
                for i in range(2):
                    last = v.scalar_tensor_tensor(ynT[:, 6 + i, :], o5[:, i, :], sm("gng")[:, 6 + i:7 + i], rstd, ALU.mult, ALU.mult)
                link(last)

                def maxima(n):
                    grp, i = n // 2, n % 2
                    w = (i + 1) * P
                    at = 0 if i == 0 else P
                    u = 6 * l + n
                    dve.wait_ge(logits_ready, u + 1)
                    if n == 0:
                        dve.wait_ge(mc_ready, l + 1)
                    m = [mC[:, :, at:at + w], causal[:, at:at + w].unsqueeze(1).broadcast_to([P, HEADS, w]),
                         mA[:, :, at:at + w]][grp]
                    if n >= 2:
                        dve.wait_ge(pt_ready, (u - 1) * 2)
                    v.tensor_tensor(soft[:, i, :, 0:w], pair((n + 1) % 2).rearrange("p (q s) -> p q s", q=HEADS)[:, :, 0:w],
                                    m, ALU.add).then_inc(logits_taken, 1)
                    dve.wait_ge(logits_taken, u + 1)
                    v.tensor_reduce(nmx[:, 4 * i:4 * i + 4], soft[:, i, :, 0:w], AX_X, ALU.max, negate=True)\
                        .then_inc(max_ready, 1)

                def outputs(n):
                    i = n % 2
                    u = 6 * l + n
                    dve.wait_ge(probs_ready, u + 1)
                    link(v.reciprocal(rs[:, 4 * i:4 * i + 4], sums[:, 4 * i:4 * i + 4]))
                    dve.wait_ge(pv_done, u + 1)
                    y3 = yrow[:, i, :].rearrange("p (h d) -> p h d", h=HEADS)
                    if n >= 2:
                        dve.wait_ge(region_filled, l * N_REG + REG_POS[f"yt{n - 2}"] + 1)
                    v.tensor_tensor(y3, bank[:, 6 + i, 0:GW].rearrange("p (h d) -> p h d", h=HEADS),
                                    rs[:, 4 * i:4 * i + 4].unsqueeze(2).broadcast_to([P, HEADS, HD]), ALU.mult)\
                        .then_inc(pv_taken, 1)
                    dve.wait_ge(pv_taken, u + 1)
                    v.tensor_tensor_reduce(wk[:, 0:GW], yrow[:, i, :], yrow[:, i, :], 1.0 / GW, EPS, ALU.mult, ALU.add,
                                           yss[:, i:i + 1]).then_inc(yss_ready, 1)
                    dve.wait_ge(yrs_ready, u + 1)
                    v.tensor_scalar(yrow[:, i, :], yrow[:, i, :], yrs[:, i:i + 1], None, ALU.mult).then_inc(yn_ready, 1)

                for n in range(6):
                    maxima(n)
                    if n:
                        outputs(n - 1)
                outputs(5)
                for m in range(KT):
                    v.scalar_tensor_tensor(xT[:, m, :], take(l, f"out{m}"), mod2[:, l, 2 * KT + m:2 * KT + m + 1], xT[:, m, :],
                                           ALU.mult, ALU.add).then_inc(dve_taken, 1)
                dve.wait_ge(dve_taken, taken_count(l, f"out{KT - 1}")[1])
                normed(l, "ss2")
                for k in range(KT):
                    dve.wait_ge(h_ready, 2 * KT * l + KT + k + 1)
                    link(v.tensor_copy(h_hi[:, k, :], sq[:, k, :]))
                    v.tensor_tensor(h_lo[:, k, :], sq[:, k, :], h_hi[:, k, :].bitcast(F32), ALU.subtract).then_inc(h_split, 1)
                dve.wait_ge(h_split, (l + 1) * KT)
                for i in range(TT):
                    for h in range(PH):
                        if i == 0:
                            dve.wait_ge(act_taken, taken_count(l, f"sc{h}_1")[1])
                        for w in range(2):
                            s = scores[:, i * PH + h, w * P:w * P + P]
                            vv, ii = vals[:, h, w, :], idxu[:, h, w, :]
                            link(v.max(vv[:, 0:8], s))
                            v.max_index(ii[:, 0:8], vv[:, 0:8], s)
                            link(v.match_replace(wk[:, 0:P], vv[:, 0:8], s, TAKEN))
                            link(v.max(vv[:, 8:16], wk[:, 0:P]))
                            link(v.max_index(ii[:, 8:16], vv[:, 8:16], wk[:, 0:P]))
                        cand = wk[:, 0:PK * PK]
                        link(v.tensor_tensor(cand.rearrange("p (i j) -> p i j", i=PK),
                                             vals[:, h, 0, :].unsqueeze(2).broadcast_to([P, PK, PK]),
                                             vals[:, h, 1, :].unsqueeze(1).broadcast_to([P, PK, PK]), ALU.add))
                        link(v.max(vc[:, i, h, 0:8], cand))
                        link(v.max_index(icu[:, h, 0:8], vc[:, i, h, 0:8], cand))
                        link(v.match_replace(cand, vc[:, i, h, 0:8], cand, TAKEN))
                        link(v.max(vc[:, i, h, 8:16], cand))
                        link(v.max_index(icu[:, h, 8:16], vc[:, i, h, 8:16], cand))
                    v.tensor_copy(gsum, vc[:, i, :, 0])
                    v.tensor_copy(idxf[:, :, :, :], idxu[:, :, :, :])
                    link(v.tensor_scalar(icu2[:, :, :], icu[:, :, :], 4, None, ALU.logical_shift_right))
                    link(v.tensor_copy(icf[:, 0, :, :], icu2[:, :, :]))
                    link(v.tensor_scalar(icu2[:, :, :], icu[:, :, :], PK - 1, None, ALU.bitwise_and))
                    link(v.tensor_copy(icf[:, 1, :, :], icu2[:, :, :]))
                    v.tensor_tensor(vc[:, i, :, :], vc[:, i, :, :], gsum.unsqueeze(2).broadcast_to([P, PH, PK]), ALU.subtract)\
                        .then_inc(gate_max, 1)
                    hot = onehot.rearrange("p (h k j) -> p h k j", h=PH, k=PK)
                    hot3 = onehot.rearrange("p (n j) -> p n j", j=PK)
                    for w in range(2):
                        link(v.tensor_tensor(hot3, icf[:, w, :, :].rearrange("p h k -> p (h k)").unsqueeze(2).broadcast_to([P, P, PK]),
                                             iota[:, 0:PK].unsqueeze(1).broadcast_to([P, P, PK]), ALU.is_equal))
                        for h in range(PH):
                            last = v.tensor_tensor(hot[:, h, :, :], hot[:, h, :, :],
                                                   idxf[:, h, w, :].unsqueeze(1).broadcast_to([P, PK, PK]), ALU.mult)
                        link(last)
                        link(v.tensor_reduce(res[:, i, w, :], hot3, AX_X, ALU.add))
                for i in range(TT):
                    dve.wait_ge(gate_exp, TT * l + i + 1)
                    link(v.tensor_reduce(gsum, vc[:, i, :, :], AX_X, ALU.add))
                    link(v.reciprocal(gsum, gsum))
                    v.tensor_tensor(res[:, i, 2, :].rearrange("p (h k) -> p h k", h=PH), vc[:, i, :, :],
                                    gsum.unsqueeze(2).broadcast_to([P, PH, PK]), ALU.mult).then_inc(picked, 1)
                    dve.wait_ge(picked, TT * l + i + 1)
                dve.wait_ge(pick_ready, TT * (l + 1))
                g3 = grid[:, :].rearrange("p (a t) -> p a t", a=KEYS)

                def one_hots(n, j):
                    v.tensor_tensor(hotB[j][:, 0:2, :], iota.unsqueeze(1).broadcast_to([P, 2, P]),
                                    pick[:, 1, bass.ds(n * 8, 2)].unsqueeze(2).broadcast_to([P, 2, P]), ALU.is_equal)
                    v.tensor_tensor(hotA[j], iota.unsqueeze(1).broadcast_to([P, 8, P]),
                                    pick[:, 0, bass.ds(n * 8, 8)].unsqueeze(2).broadcast_to([P, 8, P]), ALU.is_equal).then_inc(hot_eq, 1)

                def weigh(t, b):
                    gw = g3[:, :, bass.ds(t, 4)]
                    v.tensor_tensor(gw, gw, bank[:, b, :].rearrange("p (t a) -> p a t", t=4), ALU.mult).then_inc(w_ready, 1)

                quads = T // 4
                q0 = quads * l
                one_hots(0, 0)
                dve.wait_ge(gelu_done, KEYS // 2 * (l + 1))
                one_hots(1, 1)
                with dve.Fori(0, quads // 4 - 1, 1) as i:
                    for j in range(4):
                        dve.wait_ge(g_ready, i * 4 + (q0 + j + 1))
                        weigh(i * 16 + 4 * j, j)
                        if j % 2:
                            one_hots(i * 2 + (2 + j // 2), j // 2)
                for n in range(quads - 4, quads):
                    dve.wait_ge(g_ready, q0 + n + 1)
                    weigh(4 * n, n % 4)
                dve.wait_ge(w_ready, quads * (l + 1))
                late = early_at(l) + EARLY
                for j in range(SPLIT):
                    dve.wait_ge(vhi_ready, l * KEYS + j + 1)
                    v.tensor_tensor(w_lo[:, j, :], grid[:, j * T:j * T + T], w_hi[:, j, :].bitcast(F32), ALU.subtract).then_inc(v_ready, 1)

                def lows():
                    with dve.Fori(0, LATE // SPLIT, 1) as i:
                        for j in range(SPLIT):
                            dve.wait_ge(vhi_ready, i * SPLIT + (l * KEYS + SPLIT + j + 1))
                            v.tensor_tensor(split_lo[:, j, :], ring[:, (late + j) % RING, :], split_hi[:, j, :].bitcast(F32), ALU.subtract)
                            v.tensor_tensor(w_lo[:, j, :], grid[:, bass.ds(i * (SPLIT * T) + (SPLIT + j) * T, T)],
                                            w_hi[:, j, :].bitcast(F32), ALU.subtract).then_inc(v_ready, 1)

                lows()
                if l + 1 < DEPTH:
                    add_biases(l + 1, 0)
                dve.wait_ge(v_used, (l + 1) * KEYS)
                for m in range(KT):
                    v.scalar_tensor_tensor(xT[:, m, :], bank[:, 4 + m // 2, (m % 2) * T:(m % 2) * T + T],
                                           mod2[:, l, 5 * KT + m:5 * KT + m + 1], xT[:, m, :], ALU.mult, ALU.add).then_inc(x_done, 1)
                dve.wait_ge(x_done, (l + 1) * KT)
            dve.wait_ge(act_taken, DEPTH * PER_TAKER["act"] + 1)
            link(v.reciprocal(rstd, rstd))
            f0 = VEC_AT["fg"][0]
            for m in range(KT):
                last = v.scalar_tensor_tensor(hT[:, m, :], xT[:, m, :], V[:, f0 + m:f0 + m + 1], rstd, ALU.mult, ALU.mult)
            last.then_inc(out_ready, 1)

        @block.tensor
        def _(pe):
            mm = nc.tensor.matmul
            n_block = [0]
            to_free = [0]

            def free_block(first):
                if to_free[0]:
                    first.then_inc(block_used, to_free[0])
                    to_free[0] = 0

            n_block[0] = ADA

            def load():
                n = n_block[0]
                n_block[0] += 1
                pe.wait_ge(slot_filled[n % RING], 16 * (n // RING + 1))
                return ring[:, n % RING, :].rearrange("p (k c) -> p k c", k=KT)

            def free_region(l, name):
                p = l * N_REG + REG_POS[name]
                if p >= 2:
                    w, c = taken_count((p - 2) // N_REG, REGIONS[(p - 2) % N_REG][0])
                    pe.wait_ge(act_taken if w == "act" else dve_taken, c)
                return region(p)

            def project(l, name, rhs, cols=slice(0, P), rows=slice(0, P)):
                b = load()
                r = free_region(l, name)
                for k in range(KT):
                    last = mm(r[:, :], b[:, k, :], rhs[:, k, :], start=(k == 0), stop=(k == KT - 1))
                return last

            def sums_of(l, name, src, n, squares=None):
                r = free_region(l, name)
                for k in range(n):
                    if squares is not None:
                        pe.wait_ge(sq_ready, squares + k + 1)
                    last = mm(r, ones, src[:, k, :], start=(k == 0), stop=(k == n - 1))
                    if k == 0 and n > 1:
                        free_block(last)
                last.then_inc(region_filled, 1)

            def ada_sums(b, i, acc):
                for m in range(KT):
                    last = mm(bank[:, b, bass.ds(i * KT + m, 1)], acc[:, m * P:m * P + P], ones[:, 0:1], start=True, stop=True)
                last.then_inc(ada_columns, 1)

            pe.wait_ge(const_in, 16)

            def add_bucket(b, slot, j):
                pe.wait_ge(ge_ready, b + 1)
                pe.wait_ge(diag_ready, b + 1)
                for q in range(HEADS):
                    for part in range(2):
                        last = mm(bank[:, 2 + q, 0:P + T], diag[:, j, q, part, :], ge[:, slot, :],
                                  start=isinstance(b, int) and b + part == 0, stop=False, skip_group_check=True)
                last.then_inc(bucket_added, 1)

            for b in range(FIRST):
                add_bucket(b, b, b % 2)
            with pe.Fori(0, ADA // KT, 1) as i:
                for k in range(4):
                    add_bucket(i * 4 + (FIRST + k), k, (FIRST + k) % 2)
            for i in range(ADA // KT):
                pe.wait_ge(ada_used, i * KT + KT)
                acc = g(ACC0 + i * BLOCK, BLOCK)
                ada_sums(7, i, acc)
            pe.wait_ge(zero_ready, 1)
            for l in range(DEPTH):
                if l:
                    pe.wait_ge(x_done, l * KT)
                    n_block[0] = mix_at(l)
                pe.wait_ge(const_in, 16)
                sums_of(l, "ss1", sq, KT, 2 * KT * l)
                pe.wait_ge(h_ready, 2 * KT * l + KT)

                def transposed(name):
                    b = load()
                    r = free_region(l, name)
                    for k in range(KT):
                        last = mm(r, b[:, k, :], hT[:, k, :], start=(k == 0), stop=(k == KT - 1))
                        if k == 0:
                            free_block(last)
                    last.then_inc(region_filled, 1)
                    to_free[0] += 1

                def by_rows(name):
                    b = load()
                    r = free_region(l, name)
                    for i in range(TT):
                        for k in range(KT):
                            last = mm(r[:, i * P:i * P + P], hT[:, k, i * P:i * P + P], b[:, k, :], start=(k == 0), stop=(k == KT - 1))
                            if k == 0:
                                free_block(last)
                    last.then_inc(region_filled, 1)
                    to_free[0] += 1

                def s5_inputs(m):
                    b = load()
                    if m:
                        pe.wait_ge(bu_taken, 2 * l + m)
                    pe.wait_ge(act_taken, taken_count(l, "du1")[1])
                    for part in range(2):
                        for j in range(4):
                            last = mm(pair(part)[:, j * T:j * T + T], b[:, 4 * part + j, :], du[:, m, :], start=True, stop=True)
                            if j == 0:
                                free_block(last)
                    last.then_inc(bu_ready, 1)
                    to_free[0] += 1

                for n in ("du0", "du1", "iq0", "iq1", "ik"):
                    transposed(n)
                s5_inputs(0)
                for n in ("aq0", "aq1", "ak0", "ak1"):
                    transposed(n)
                s5_inputs(1)
                by_rows("av0")
                by_rows("av1")
                r = free_region(l, "iwcf")
                w8 = small_of(l, "iwcf").rearrange("p (k c) -> p k c", k=KT)
                pe.wait_ge(small_in, 16)
                for i in range(TT):
                    for k in range(KT):
                        last = mm(r[:, i * 8:i * 8 + 8], hT[:, k, i * P:i * P + P], w8[:, k, :], start=(k == 0), stop=(k == KT - 1))
                last.then_inc(region_filled, 1)

                def head_logits(w, i, q_of, k_of):
                    n = (i + 1) * P
                    for q in range(HEADS):
                        h = PERM[q]
                        last = mm(pair(w)[:, q * T:q * T + n], q_of(h)[:, i * P:i * P + P], k_of(h)[:, 0:n], start=True, stop=True)
                    return last

                def half(t, h):
                    lo = (h % 2) * HD
                    return t[lo:lo + HD]

                pe.wait_ge(bu_taken, 2 * (l + 1))
                pe.wait_ge(act_taken, taken_count(l, "ik")[1])
                for i in range(TT):
                    head_logits(i, i, lambda h: half(iq[:, h // 2, :], h), lambda h: half(ik, h)).then_inc(dots_ready, 1)
                for n in ("cq0", "cq1", "ckv"):
                    transposed(n)
                b = load()
                for w, name in enumerate(("krA", "krB")):
                    r = free_region(l, name)
                    for k in range(KT):
                        last = mm(r[64:P], b[:, k, 64 * w:64 * w + 64], hT[:, k, :], start=(k == 0), stop=(k == KT - 1))
                        if k == 0:
                            free_block(last)
                    last.then_inc(region_filled, 1)
                to_free[0] += 1
                transposed("fq0")
                pe.wait_ge(sqB_ready, l + 1)
                sums_of(l, "ssq", sqB, 2)
                sums_of(l, "sskv", sqB[:, 2:3, :], 1)
                for n in ("fq1", "fk0", "fk1"):
                    transposed(n)
                by_rows("fv0")
                by_rows("fv1")
                pe.wait_ge(logf_ready, l + 1)
                r = free_region(l, "fcum")
                lg = logf.rearrange("p (j h) -> p j h", j=TT)
                for i in range(TT):
                    for j in range(i + 1):
                        last = mm(r[:, i * HEADS:i * HEADS + HEADS], utri[:, j, i * P:i * P + P], lg[:, j, :], start=(j == 0), stop=(j == i))
                last.then_inc(region_filled, 1)
                pe.wait_ge(relu_ready, TT * (l + 1))
                for h in range(HEADS):
                    for j in range(TT):
                        last = mm(pair(0)[:, h * T:h * T + T], nlogf[:, j, h, :], utri[:, j, :], start=(j == 0), stop=(j == TT - 1))
                last.then_inc(cb_ready, 1)
                pe.wait_ge(latent_ready, l + 1)
                b = load()
                wq = b.rearrange("p k c -> p (k c)").rearrange("p (k h c) -> p k h c", k=2, h=HEADS)
                for h in range(HEADS):
                    r = free_region(l, f"qB{h}")
                    for k in range(2):
                        last = mm(r, wq[:, k, h, :], cqn[:, k, :], start=(k == 0), stop=(k == 1))
                        if k == 0:
                            free_block(last)
                    last.then_inc(region_filled, 1)
                to_free[0] += 1
                b = load()
                wkv = b.rearrange("p k c -> p (k c)")
                for h in range(HEADS):
                    r = free_region(l, f"kB{h}")
                    mm(r[0:NOPE], wkv[:, h * NOPE:h * NOPE + NOPE], ckvn, start=True, stop=True).then_inc(region_filled, 1)
                for i in range(TT):
                    r = free_region(l, f"vB{i}")
                    mm(r, ckvn[:, i * P:i * P + P], wkv[:, GW:2 * GW], start=True, stop=True).then_inc(region_filled, 1)
                to_free[0] += 1
                pe.wait_ge(re_ready, l + 1)
                pe.wait_ge(im_ready, l + 1)
                for m in range(2):
                    r = free_region(l, f"y5_{m}")
                    for j in range(4):
                        jj = 4 * m + j
                        for c, (w, x5) in enumerate(((csre, vre), (csim, vim))):
                            last = mm(r[C5 * j:C5 * j + C5], w[:, jj, :], x5[:, jj * T:jj * T + T], start=(c == 0), stop=(c == 1))
                    last.then_inc(region_filled, 1)
                pe.wait_ge(g5_ready, 2 * (l + 1))
                for m in range(2):
                    r = free_region(l, f"glu{m}")
                    for k in range(2):
                        last = mm(r, wglu[:, k, m * P:m * P + P], g5[:, k, :], start=(k == 0), stop=(k == 1))
                    last.then_inc(region_filled, 1)
                pe.wait_ge(sq5_ready, l + 1)
                sums_of(l, "ss5", sg5, 2)

                def logits(n):
                    grp, i = n // 2, n % 2
                    u = 6 * l + n
                    if n == 0:
                        pe.wait_ge(act_taken, taken_count(l, "fk1")[1])
                        pe.wait_ge(relu_ready, TT * (l + 1))
                    if n == 1:
                        pe.wait_ge(mc_ready, l + 1)
                    if n >= 2:
                        pe.wait_ge(pt_taken, (u - 1) * 2)
                    if n == 2:
                        pe.wait_ge(act_taken, taken_count(l, "kB3")[1])
                        pe.wait_ge(dve_taken, taken_count(l, "qB3")[1])
                        pe.wait_ge(kr_ready, l + 1)
                    qo, ko = [(lambda h: half(fq[:, h // 2, :], h), lambda h: half(fk[:, h // 2, :], h)),
                              (lambda h: qB[:, h, :], lambda h: kB[:, h, :]),
                              (lambda h: half(aq[:, h // 2, :], h), lambda h: half(ak[:, h // 2, :], h))][grp]
                    head_logits((n + 1) % 2, i, qo, ko).then_inc(logits_ready, 1)

                def weighted(n):
                    grp, i = n // 2, n % 2
                    u = 6 * l + n
                    val = [fv, vB, av][grp]
                    pe.wait_ge(probs_ready, u + 1)
                    for b2 in range(2):
                        for q in (2 * b2, 2 * b2 + 1):
                            for j in range(i + 1):
                                last = nc.tensor.transpose(turned((n + 1) % 2)[:, q, j, :], soft[:, i, q, j * P:j * P + P], ident)
                        last.then_inc(pt_ready, 1)
                    for q in range(HEADS):
                        h = PERM[q]
                        if q % 2 == 0:
                            pe.wait_ge(pt_taken, u * 2 + q // 2 + 1)
                        if q == 0 and u >= 2:
                            pe.wait_ge(pv_taken, u - 1)
                        for j in range(i + 1):
                            last = mm(bank[:, 6 + i, h * HD:h * HD + HD], pT[:, q, j, :], val[:, j, h * HD:h * HD + HD],
                                      start=(j == 0), stop=(j == i))
                    last.then_inc(pv_done, 1)

                def turn(n):
                    u = 6 * l + n
                    pe.wait_ge(yn_ready, u + 1)
                    r = free_region(l, f"yt{n}")
                    for k in range(2):
                        last = nc.tensor.transpose(r[:, k * P:k * P + P], yrow[:, n % 2, k * P:k * P + P], ident)
                    last.then_inc(region_filled, 1)

                for n in range(7):
                    if n < 6:
                        logits(n)
                    if n:
                        weighted(n - 1)
                    if n >= 2:
                        turn(n - 2)
                turn(5)
                pe.wait_ge(act_taken, taken_count(l, "yt5")[1])
                for m in range(KT):
                    b = load()
                    r = free_region(l, f"out{m}")
                    for k in range(KT):
                        last = mm(r, b[:, k, :], ynT[:, k, :], start=(k == 0), stop=(k == KT - 1))
                        if k == 0:
                            free_block(last)
                    last.then_inc(region_filled, 1)
                    to_free[0] += 1
                sums_of(l, "ss2", sq, KT, 2 * KT * l + KT)
                sk = [small_of(l, "sk1"), small_of(l, "sk2")]

                def exact(dst, hi, lo, x_hi, x_lo, start, stop, group=True):
                    mm(dst, hi, x_hi, start=start, stop=False, skip_group_check=not group)
                    mm(dst, hi, x_lo, start=False, stop=False, skip_group_check=not group)
                    return mm(dst, lo, x_hi, start=False, stop=stop, skip_group_check=not group)

                def times_h(dst, s, first=False):
                    hi, lo = [t[:, s, :].rearrange("p (k c) -> p k c", k=KT) for t in (split_hi, split_lo)]
                    for k in range(KT):
                        if first:
                            pe.wait_ge(h_split, l * KT + k + 1)
                        last = exact(dst, hi[:, k, :], lo[:, k, :], h_hi[:, k, :], h_lo[:, k, :], k == 0, k == KT - 1)
                    return last

                def keys(h):
                    pe.wait_ge(act_taken, taken_count(l, f"pq{h}_1")[1])
                    for i in range(TT):
                        r = free_region(l, f"sc{h}_{i}")
                        for w in range(2):
                            last = mm(r[:, w * P:w * P + P], qT[:, 2 * (h % 2) + w, i * P:i * P + P], sk[w], start=True, stop=True)
                        last.then_inc(region_filled, 1)

                for h in range(PH + 1):
                    for w in range(2):
                        if h < PH:
                            pe.wait_ge(lo_ready, l * EARLY + 2 * h + w + 1)
                            times_h(free_region(l, f"pq{h}_{w}"), (2 * h + w) % SPLIT, first=(h + w == 0)).then_inc(region_filled, 1)
                    if h:
                        keys(h - 1)
                pe.wait_ge(act_taken, taken_count(l, f"sc{PH - 1}_1")[1])
                pairs = KEYS // 2 * l

                def expert_rows(i, first_turn):
                    for j in range(8):
                        pe.wait_ge(lo_ready, i * 8 + (l * EARLY + PQ + j + 1))
                        if j % 2 == 0 and not first_turn:
                            pe.wait_ge(gelu_done, i * 4 + (pairs + j // 2 - 3))
                        last = times_h(bank[:, j // 2, (j % 2) * T:(j % 2) * T + T], (PQ + j) % SPLIT)
                        if j % 2:
                            last.then_inc(a_ready, 1)

                expert_rows(0, True)
                with pe.Fori(1, 13, 1) as i:
                    expert_rows(i, False)
                pe.wait_ge(pv_taken, 6 * (l + 1))
                pe.wait_ge(picked, TT * (l + 1))
                for i in range(TT):
                    for r3 in range(3):
                        last = nc.tensor.transpose(bank[:, 6 + i, r3 * P:r3 * P + P], res[:, i, r3, :], ident)
                last.then_inc(turned_picks, 1)
                with pe.Fori(13, KEYS // 8, 1) as i:
                    expert_rows(i, False)
                pe.wait_ge(gelu_done, KEYS // 2 * (l + 1))
                quads = T // 4
                q0 = quads * l

                def gate_grids(i, j, first_turn):
                    pe.wait_ge(hot_ready, i * 2 + (T // 8 * l + j // 2 + 1))
                    pe.wait_ge(column_ready, i * 2 + (T // 8 * l + j // 2 + 1))
                    if not first_turn:
                        pe.wait_ge(w_ready, i * 4 + (q0 + j - 3))
                    for t in range(4):
                        s = 4 * (j % 2) + t
                        last = mm(bank[:, j, t * P:t * P + P], hotB[j // 2][:, s, :], hotA[j // 2][:, s, :], start=True, stop=True)
                    last.then_inc(g_ready, 1)

                for j in range(4):
                    gate_grids(0, j, True)
                with pe.Fori(1, quads // 4, 1) as i:
                    for j in range(4):
                        gate_grids(i, j, False)
                pe.wait_ge(w_ready, quads * (l + 1))
                pe.wait_ge(lo_ready, (l + 1) * EARLY)
                for b4 in range(4):
                    for hf in range(2):
                        mm(bank[:, 4 + b4, hf * T:hf * T + T], zeros[:, :], xT[:, 0, :], start=(hf == 0), stop=False,
                           skip_group_check=True)

                def output_rows(i, n, a0):
                    for j in range(n):
                        s = (a0 + j) % SPLIT
                        pe.wait_ge(v_ready, i * n + (l * KEYS + a0 + j + 1))
                        for m in range(KT):
                            c = slice(m * P, m * P + P)
                            last = exact(bank[:, 4 + m // 2, (m % 2) * T:(m % 2) * T + T], split_hi[:, s, c], split_lo[:, s, c],
                                         w_hi[:, s, :], w_lo[:, s, :], False, False, group=False)
                        last.then_inc(v_used, 1)

                if l + 1 < DEPTH:
                    with pe.Fori(0, ADA // KT, 1) as i:
                        output_rows(i, 20, 0)
                        pe.wait_ge(ada_used, i * KT + ((l + 1) * ADA + KT))
                        ada_sums(0, i, ada_acc)
                    output_rows(0, 8, 120)
                else:
                    with pe.Fori(0, KEYS // SPLIT, 1) as i:
                        output_rows(i, SPLIT, 0)
            w, c = taken_count(DEPTH - 1, REGIONS[-1][0])
            pe.wait_ge(act_taken, c)
            for k in range(KT):
                pe.wait_ge(sq_ready, 2 * KT * DEPTH + k + 1)
                last = mm(bank[:, 0, 0:T], ones, sq[:, k, :], start=(k == 0), stop=(k == KT - 1))
            last.then_inc(region_filled, 1)


def column_block(w):
    return w.reshape(KT, P, P).transpose(1, 0, 2).reshape(P, BLOCK)


def swapped(w):
    return np.concatenate([w[:, ROPE // 2:], w[:, :ROPE // 2]], axis=1)


def layer_blocks(i, l, dst):
    n = 0
    w_in = i["w_in"][l]

    def cols(name):
        return w_in[:, IN_AT[name][0]:IN_AT[name][1]]

    kr = cols("b_kr")
    wide = {"du": cols("d_u"), "iq": cols("i_q"), "aq": cols("a_q"), "ak": cols("a_k"), "av": cols("a_v"),
            "cq": cols("b_cq"), "fq": cols("c_q"), "fk": cols("c_k"), "fv": cols("c_v")}
    for name in MIX_BLOCKS:
        if name == "ik":
            b = column_block(np.concatenate([cols("i_k"), cols("i_k")], axis=1))
        elif name == "ckv":
            b = column_block(cols("b_ckv"))
        elif name == "kr":
            b = column_block(np.concatenate([kr, kr, swapped(kr), swapped(kr)], axis=1))
        elif name in ("B0", "B1"):
            m = int(name[1])
            b = np.zeros((P, 2, 4, P), np.float32)
            for part, w in enumerate((i["s5_B_re"][l], i["s5_B_im"][l])):
                for gg in range(8):
                    s = (gg % 2) * 64
                    b[gg * 16:gg * 16 + 16, part, gg // 2, s:s + 64] = w[8 * m + gg].T
            b = b.reshape(P, BLOCK)
        elif name == "UQ":
            w = i["mla_w_uq"][l].reshape(2, P, HEADS, NOPE + ROPE)
            x1, x2 = w[..., NOPE:NOPE + ROPE // 2], w[..., NOPE + ROPE // 2:]
            b = np.concatenate([w, x2, x1], axis=-1).transpose(1, 0, 2, 3).reshape(P, BLOCK)
        elif name == "UKV":
            w = i["mla_w_ukv"][l].reshape(KV_RANK, HEADS, 2, HD).transpose(0, 2, 1, 3).reshape(KV_RANK, 2 * GW)
            b = np.concatenate([w, np.zeros((P, BLOCK - 2 * GW), np.float32)], axis=1)
        else:
            k = int(name[2])
            b = column_block(wide[name[:2]][:, k * P:k * P + P])
        dst[n] = b
        n += 1
    for m in range(KT):
        dst[n] = column_block(i["w_out"][l][:, m * P:m * P + P])
        n += 1
    for m in range(PQ):
        dst[n] = column_block(i["peer_w_q"][l][:, m * P:m * P + P])
        n += 1
    dst[n:n + KEYS] = i["peer_u"][l].reshape(KEYS, P, KT, P).transpose(0, 3, 2, 1).reshape(KEYS, P, BLOCK)
    n += KEYS
    dst[n:n + KEYS] = i["peer_v"][l].reshape(KEYS, P, BLOCK)


def small_columns(i, l):
    s = np.zeros((P, N_SMALL), np.float32)

    def put(name, a):
        s[:, SMALL_AT[name][0]:SMALL_AT[name][1]] = a

    def feat(v):
        return v.reshape(-1, P).T

    put("n1g", feat(i["norm1_g"][l]))
    put("n2g", feat(i["norm2_g"][l]))
    put("adab", feat(i["ada_b"][l]))
    put("qg", feat(i["mla_q_norm_g"][l]))
    put("kvg", feat(i["mla_kv_norm_g"][l]))
    put("gng", feat(i["group_norm_g"][l]))
    put("lre", feat(i["s5_A_re"][l].reshape(-1)))
    put("lim", feat(i["s5_A_im"][l].reshape(-1)))
    put("ldt", feat(np.repeat(i["s5_log_dt"][l], 64)))
    put("D", feat(i["s5_D"][l]))
    put("bglu", feat(i["s5_b_glu"][l]))
    w = i["w_in"][l]
    w8 = np.concatenate([w[:, IN_AT["i_w"][0]:IN_AT["i_w"][1]], w[:, IN_AT["c_f"][0]:IN_AT["c_f"][1]]], axis=1)
    put("iwcf", w8.reshape(KT, P, 8).transpose(1, 0, 2).reshape(P, KT * 8))
    put("bf", np.broadcast_to(i["fox_b_f"][l][None, :], (P, HEADS)))
    put("sk1", i["peer_subkeys1"][l].T)
    put("sk2", i["peer_subkeys2"][l].T)
    return s


def s5_columns(i, l):
    s = np.zeros((P, 1024), np.float32)
    for part, w in enumerate((i["s5_C_re"][l], i["s5_C_im"][l])):
        for gg in range(16):
            j, r = gg // 2, (gg % 2) * 64
            at = part * 256 + j * C5 + (gg % 2) * 16
            s[r:r + 64, at:at + 16] = w[gg].T
    s[:, 512:] = i["s5_w_glu"][l].reshape(2, P, GW).transpose(1, 0, 2).reshape(P, 512)
    return s


def kernel(**inputs):
    import concourse.bacc as _bacc
    from concourse.bass_utils import run_bass_kernel_spmd as _run

    i = {n: np.asarray(v) for n, v in inputs.items()}
    stream = np.empty((N_BLOCKS, P, BLOCK), np.float32)
    for l in range(DEPTH):
        at = N_MAIN + (l - 1) * ADA if l else 0
        stream[at:at + ADA] = i["ada_w"][l].reshape(KT, P, ADA // KT, BLOCK).transpose(2, 0, 1, 3).reshape(ADA, P, BLOCK)
        at = ADA + l * LAYER_BLOCKS
        layer_blocks(i, l, stream[at:at + LAYER_BLOCKS])
    s5w = np.stack([s5_columns(i, l) for l in range(DEPTH)])
    small = np.stack([small_columns(i, l) for l in range(DEPTH)], axis=1)
    vec = np.concatenate([i["c"].reshape(KT, P).T, i["final_g"].reshape(KT, P).T,
                          np.broadcast_to(i["rel_bias"].reshape(1, -1), (P, BUCKETS * HEADS))], axis=1)
    p = i["positions"].reshape(T)
    pos = np.concatenate([np.broadcast_to(p[None, :], (P, T)), p.reshape(TT, P).T], axis=1)
    x = i["x"].reshape(T, KT, P).transpose(2, 1, 0)
    consts, mixc = constants()
    arrays = {"stream": stream, "s5w": s5w, "consts": consts, "mixc": mixc, "small": small, "vec": vec, "pos": pos, "x_in": x}
    arrays = {n: np.ascontiguousarray(a) for n, a in arrays.items()}
    nc = _bacc.Bacc("TRN2", target_bir_lowering=False, num_devices=1, dynamic_dma_scratch_size=1024)
    args = [nc.dram_tensor(n, a.shape, mybir.dt.from_np(a.dtype), kind="ExternalInput").ap() for n, a in arrays.items()]
    args.append(nc.dram_tensor("y_out", (P, KT, T), F32, kind="ExternalOutput").ap())
    build(nc, *args)
    r = _run(nc, [arrays], core_ids=[0])
    y = r.results[0]["y_out"]
    return y.transpose(2, 1, 0).reshape(1, T, D)
```
